# Optimizing a Trainium2 kernel written in Bass

```python
import jax, jax.numpy as jnp
from jax import lax
import numpy as np

D_MODEL = 2048
BATCH = 1
SEQ = 256
DEPTH = 2
DEC_BATCH = 8
DEC_SEQ = 8
PAST_LEN = 2048
PAGE_SIZE = 128

N_MIXERS = 2
N_DELTA_LAYERS = (DEPTH + 1) // N_MIXERS
N_POOL_LAYERS = DEPTH // N_MIXERS
EXPAND = 2
D_INNER = EXPAND * D_MODEL
HEAD_DIM = 128
N_QK_HEADS = D_MODEL // HEAD_DIM
N_V_HEADS = D_INNER // HEAD_DIM
QK_DIM = N_QK_HEADS * HEAD_DIM
CONV_WIDTH = 4
CONV_DIM = 2 * QK_DIM + D_INNER
DELTA_IN_DIM = CONV_DIM + D_INNER + 2 * N_V_HEADS
CHUNK = 64
POOL_WINDOWS = (2, 4, 8, 16)
N_POOL_GROUPS = len(POOL_WINDOWS)
POOL_GROUP_DIM = D_INNER // N_POOL_GROUPS
POOL_BUF = max(POOL_WINDOWS) - 1
NORM_EPS = 1e-6

kernel_name = 'hybrid_gated_delta_pool_decoder_step'

def rmsnorm(x, w):
    xf = x.astype(jnp.float32)
    y = xf * lax.rsqrt(jnp.mean(xf * xf, axis=-1, keepdims=True) + NORM_EPS)
    return (y * w.astype(jnp.float32)).astype(x.dtype)

def l2norm(x):
    return x * lax.rsqrt(jnp.sum(x * x, axis=-1, keepdims=True) + NORM_EPS)

def causal_conv(x, buf, w):
    t = x.shape[1]
    xp = jnp.concatenate([buf.astype(x.dtype), x], axis=1)
    y = w[0] * xp[:, 0:t]
    for j in range(1, CONV_WIDTH):
        y = y + w[j] * xp[:, j:j + t]
    return jax.nn.silu(y), xp[:, -(CONV_WIDTH - 1):].astype(buf.dtype)

def _to_chunks(a, n, c):
    b, t = a.shape[:2]
    a = jnp.pad(a, [(0, 0), (0, n * c - t)] + [(0, 0)] * (a.ndim - 2))
    a = a.reshape((b, n, c) + a.shape[2:])
    return jnp.transpose(a, (1, 0, 3, 2) + tuple(range(4, a.ndim)))

def gated_delta_rule(q, k, v, g, beta, s0):
    b, t, h, _ = q.shape
    dv = v.shape[-1]
    c = min(CHUNK, t)
    n = -(-t // c)
    q, k, v = _to_chunks(q, n, c), _to_chunks(k, n, c), _to_chunks(v, n, c)
    g, beta = _to_chunks(g, n, c), _to_chunks(beta, n, c)
    gc = jnp.cumsum(g, axis=-1)
    diff = gc[..., :, None] - gc[..., None, :]
    incl = jnp.tril(jnp.ones((c, c), dtype=bool))
    strict = jnp.tril(jnp.ones((c, c), dtype=bool), -1)
    decay_incl = jnp.exp(jnp.where(incl, diff, -jnp.inf))
    decay_strict = jnp.where(strict, decay_incl, 0.0)
    kb = k * beta[..., None]
    lmat = jnp.einsum('nbhcd,nbhed->nbhce', kb, k) * decay_strict
    eye = jnp.eye(c, dtype=jnp.float32)
    tmat = lax.linalg.triangular_solve(lmat + eye, jnp.broadcast_to(eye, lmat.shape),
                                       left_side=True, lower=True, unit_diagonal=True)
    u_base = jnp.einsum('nbhce,nbhef->nbhcf', tmat, v * beta[..., None])
    w_dec = jnp.einsum('nbhce,nbhed->nbhcd', tmat, kb * jnp.exp(gc)[..., None])
    qk = jnp.einsum('nbhcd,nbhed->nbhce', q, k) * decay_incl
    qg = q * jnp.exp(gc)[..., None]
    g_last = gc[..., -1]
    kdec = k * jnp.exp(g_last[..., None] - gc)[..., None]

    def step(s, xs):
        u_b, w_c, qg_c, qk_c, kd_c, gl = xs
        u = u_b - jnp.einsum('bhcd,bhde->bhce', w_c, s)
        o = jnp.einsum('bhcd,bhde->bhce', qg_c, s) + jnp.einsum('bhce,bhef->bhcf', qk_c, u)
        s = s * jnp.exp(gl)[..., None, None] + jnp.einsum('bhcd,bhce->bhde', kd_c, u)
        return s, o

    s_final, o = lax.scan(step, s0, (u_base, w_dec, qg, qk, kdec, g_last))
    o = jnp.transpose(o, (1, 0, 3, 2, 4)).reshape(b, n * c, h, dv)[:, :t]
    return o, s_final

def delta_mixer(h, s0, conv_buf, w_in, conv_w, a_log, dt_bias, o_norm_w, w_out):
    b, t, _ = h.shape
    proj = h @ w_in
    qkv, z, beta_raw, a_raw = jnp.split(
        proj, [CONV_DIM, CONV_DIM + D_INNER, CONV_DIM + D_INNER + N_V_HEADS], axis=-1)
    qkv, conv_new = causal_conv(qkv, conv_buf, conv_w)
    q, k, v = jnp.split(qkv.astype(jnp.float32), [QK_DIM, 2 * QK_DIM], axis=-1)
    rep = N_V_HEADS // N_QK_HEADS
    q = jnp.repeat(l2norm(q.reshape(b, t, N_QK_HEADS, HEAD_DIM)) * (HEAD_DIM ** -0.5), rep, axis=2)
    k = jnp.repeat(l2norm(k.reshape(b, t, N_QK_HEADS, HEAD_DIM)), rep, axis=2)
    v = v.reshape(b, t, N_V_HEADS, HEAD_DIM)
    beta = jax.nn.sigmoid(beta_raw.astype(jnp.float32))
    g = -jnp.exp(a_log.astype(jnp.float32)) * jax.nn.softplus(
        a_raw.astype(jnp.float32) + dt_bias.astype(jnp.float32))
    o, s_new = gated_delta_rule(q, k, v, g, beta, s0.astype(jnp.float32))
    o = rmsnorm(o, o_norm_w) * jax.nn.silu(z.astype(jnp.float32).reshape(b, t, N_V_HEADS, HEAD_DIM))
    out = o.reshape(b, t, D_INNER).astype(h.dtype) @ w_out
    return out, s_new.astype(s0.dtype), conv_new

def pool_mixer(h, buf, start_pos, w_in, w_group, scale, w_out):
    b, t, _ = h.shape
    proj = h @ w_in
    u, z = jnp.split(proj, [D_INNER], axis=-1)
    xp = jnp.concatenate([buf.astype(u.dtype), u], axis=1).astype(jnp.float32)
    cs = jnp.pad(jnp.cumsum(xp, axis=1), ((0, 0), (1, 0), (0, 0)))
    end = cs[:, POOL_BUF + 1:POOL_BUF + 1 + t]
    pos = start_pos + jnp.arange(t, dtype=jnp.int32)
    means = []
    for gi, win in enumerate(POOL_WINDOWS):
        sl = slice(gi * POOL_GROUP_DIM, (gi + 1) * POOL_GROUP_DIM)
        start = cs[:, POOL_BUF + 1 - win:POOL_BUF + 1 - win + t, sl]
        cnt = jnp.minimum(pos + 1, win).astype(jnp.float32)[None, :, None]
        means.append((end[..., sl] - start) / cnt)
    pooled = jnp.concatenate(means, axis=-1) - xp[:, POOL_BUF:]
    mixed = jnp.einsum('btgc,gcd->btgd', pooled.reshape(b, t, N_POOL_GROUPS, POOL_GROUP_DIM),
                       w_group.astype(jnp.float32)).reshape(b, t, D_INNER)
    y = mixed * scale.astype(jnp.float32) * jax.nn.silu(z.astype(jnp.float32))
    out = y.astype(h.dtype) @ w_out
    return out, xp[:, -POOL_BUF:].astype(buf.dtype)

def setup_inputs(seed: int = 0) -> dict:
    key = jax.random.key(seed)
    ks = jax.random.split(key, 20)
    f32 = jnp.float32
    nd, npl = N_DELTA_LAYERS, N_POOL_LAYERS
    dt = jnp.exp(jax.random.uniform(ks[7], (nd, N_V_HEADS), f32, np.log(1e-3), np.log(1e-1)))
    return {
        'x_prompt': jax.random.normal(ks[0], (BATCH, SEQ, D_MODEL), f32),
        'x_sample': jax.random.normal(ks[1], (DEC_BATCH, DEC_SEQ, D_MODEL), f32),
        'state_delta': 0.1 * jax.random.normal(ks[2], (nd, DEC_BATCH, N_V_HEADS, HEAD_DIM, HEAD_DIM), f32),
        'cache_conv': jax.random.normal(ks[3], (nd, DEC_BATCH, CONV_WIDTH - 1, CONV_DIM), f32),
        'cache_pool': jax.random.normal(ks[4], (npl, DEC_BATCH, POOL_BUF, D_INNER), f32),
        'norm_w': 1.0 + 0.02 * jax.random.normal(ks[5], (DEPTH, D_MODEL), f32),
        'final_norm_w': 1.0 + 0.02 * jax.random.normal(ks[6], (D_MODEL,), f32),
        'delta_w_in': jax.random.normal(ks[8], (nd, D_MODEL, DELTA_IN_DIM), f32) * D_MODEL ** -0.5,
        'delta_conv_w': jax.random.normal(ks[9], (nd, CONV_WIDTH, CONV_DIM), f32) * CONV_WIDTH ** -0.5,
        'delta_a_log': jnp.log(jax.random.uniform(ks[10], (nd, N_V_HEADS), f32, 1.0, 16.0)),
        'delta_dt_bias': dt + jnp.log(-jnp.expm1(-dt)),
        'delta_o_norm_w': 1.0 + 0.02 * jax.random.normal(ks[11], (nd, HEAD_DIM), f32),
        'delta_w_out': jax.random.normal(ks[12], (nd, D_INNER, D_MODEL), f32) * D_INNER ** -0.5,
        'pool_w_in': jax.random.normal(ks[13], (npl, D_MODEL, 2 * D_INNER), f32) * D_MODEL ** -0.5,
        'pool_w_group': jax.random.normal(ks[14], (npl, N_POOL_GROUPS, POOL_GROUP_DIM, POOL_GROUP_DIM), f32) * POOL_GROUP_DIM ** -0.5,
        'pool_scale': 1.0 + 0.02 * jax.random.normal(ks[15], (npl, D_INNER), f32),
        'pool_w_out': jax.random.normal(ks[16], (npl, D_INNER, D_MODEL), f32) * D_INNER ** -0.5,
    }

def reference(x_prompt, x_sample, state_delta, cache_conv, cache_pool, norm_w, final_norm_w,
              delta_w_in, delta_conv_w, delta_a_log, delta_dt_bias, delta_o_norm_w, delta_w_out,
              pool_w_in, pool_w_group, pool_scale, pool_w_out):
    bp = x_prompt.shape[0]
    s_zero = jnp.zeros((bp,) + state_delta.shape[2:], state_delta.dtype)
    c_zero = jnp.zeros((bp,) + cache_conv.shape[2:], cache_conv.dtype)
    p_zero = jnp.zeros((bp,) + cache_pool.shape[2:], cache_pool.dtype)
    hp, hs = x_prompt, x_sample
    sd_p, cc_p, cp_p, sd_s, cc_s, cp_s = [], [], [], [], [], []
    for i in range(DEPTH):
        j = i // N_MIXERS
        np_in, ns_in = rmsnorm(hp, norm_w[i]), rmsnorm(hs, norm_w[i])
        if i % N_MIXERS == 0:
            ws = (delta_w_in[j], delta_conv_w[j], delta_a_log[j], delta_dt_bias[j],
                  delta_o_norm_w[j], delta_w_out[j])
            op, sp, cp = delta_mixer(np_in, s_zero, c_zero, *ws)
            os_, ss, cs = delta_mixer(ns_in, state_delta[j], cache_conv[j], *ws)
            sd_p.append(sp); cc_p.append(cp); sd_s.append(ss); cc_s.append(cs)
        else:
            ws = (pool_w_in[j], pool_w_group[j], pool_scale[j], pool_w_out[j])
            op, pp = pool_mixer(np_in, p_zero, 0, *ws)
            os_, ps = pool_mixer(ns_in, cache_pool[j], PAST_LEN, *ws)
            cp_p.append(pp); cp_s.append(ps)
        hp = hp + op
        hs = hs + os_
    y_prompt = rmsnorm(hp, final_norm_w)
    y_sample = rmsnorm(hs, final_norm_w)
    new_state_delta_p = jnp.stack(sd_p)
    new_cache_conv_p = jnp.stack(cc_p)
    new_cache_pool_p = jnp.stack(cp_p)
    new_state_delta_s = jnp.stack(sd_s)
    new_cache_conv_s = jnp.stack(cc_s)
    new_cache_pool_s = jnp.stack(cp_s)
    return (y_prompt, y_sample, new_state_delta_p, new_cache_conv_p, new_cache_pool_p,
            new_state_delta_s, new_cache_conv_s, new_cache_pool_s)


_drawn_inputs = setup_inputs


def setup_inputs(seed=0):
    import zlib

    import numpy as np

    out = dict(_drawn_inputs(seed))
    spreads = {}
    factors = {'final_norm_w': 2.789, 'delta_o_norm_w': 4.822, 'pool_scale': 6.801}
    for name, (base, spread) in spreads.items():
        noise = np.random.default_rng([zlib.crc32(name.encode()), seed]).standard_normal(out[name].shape)
        drawn = base * np.exp(spread * noise) if base else spread * noise
        out[name] = __import__('jax').numpy.asarray(drawn.astype(out[name].dtype))
    for name, factor in factors.items():
        out[name] = (out[name] * factor).astype(out[name].dtype)
    return out
```

```python
import concourse.bass as bass
from concourse import mybir

P = 128
NPT, NSEQ, SLEN = 256, 8, 8
T = NPT + NSEQ * SLEN
DM, DI = 2048, 4096
KT = DM // P
NH = DM // P
QKV = 2 * DM + DI
TAPS = 4
SW = SLEN + TAPS - 1
S_AT = NPT + TAPS - 1
CW = S_AT + NSEQ * SW
CV = CW - (TAPS - 1)
WINDOWS = (2, 4, 8, 16)
NG = len(WINDOWS)
PB = max(WINDOWS) - 1
PSW = SLEN + PB
PS_AT = PB + NPT
PW = PS_AT + NSEQ * PSW
EPS = 1e-6
NEG = -1e30
LEVELS = 7
S_LEVELS = 3
PK = 4
LEAD = 2

F32, F32R, U8 = mybir.dt.float32, mybir.dt.float32r, mybir.dt.uint8
ALU = mybir.AluOpType
ACT = mybir.ActivationFunctionType

HEADS = 4
OUT_A = HEADS + 12 * NH
POOL = OUT_A + 64
OUT_B = POOL + 40 * NG
J_POOL = 16
J_OUT_B = J_POOL + 12 * NG

V_SCALE, V_O = 3 * KT, 5 * KT
GC, NBETA, HBETA, NBE, EGC, DEC = (5 * k for k in range(6))
EGL = 30


def build(nc, x_prompt, x_sample, state_delta, cache_conv, cache_pool, norm_w, final_norm_w, delta_w_in,
          delta_conv_w, delta_a_log, delta_dt_bias, delta_o_norm_w, delta_w_out, pool_w_in, pool_w_group,
          pool_scale, pool_w_out, y_prompt, y_sample, new_sd_p, new_cc_p, new_cp_p, new_sd_s, new_cc_s, new_cp_s):
    def place(at, name, shape, dt=F32):
        size = 1 if dt == U8 else 4
        for n in shape:
            size *= n
        t = nc.alloc_sbuf_tensor_at(name, [P] + list(shape), dt, offset=at[0])
        at[0] += (size + 31) // 32 * 32
        return t

    m = [(nc.sbuf_base + 31) // 32 * 32]
    xhi = place(m, "xhi", [KT, T], F32R)
    xlo = place(m, "xlo", [KT, T], F32R)
    wraw = place(m, "wraw", [4, PK * 256])
    whi = place(m, "whi", [4, PK * 256], F32R)
    wlo = place(m, "wlo", [4, PK * 256], F32R)
    branch = place(m, "branch", [2 * KT, T])
    ident = place(m, "ident", [P])
    ones = place(m, "ones", [P])
    mask_p = place(m, "mask_p", [P])
    mask_s = place(m, "mask_s", [P])
    level = place(m, "level", [LEVELS, P], U8)
    seqmask = place(m, "seqmask", [NSEQ])
    minushalf = place(m, "minushalf", [8])
    vecs = place(m, "vecs", [96])
    convw = place(m, "convw", [NH, 4, TAPS])
    table = place(m, "table", [NH, 50])
    small = place(m, "small", [64])
    shared = m[0]

    a = [shared]
    convin = place(a, "convin", [4, CW])
    zraw = place(a, "zraw", [2, T])
    cc_in = place(a, "cc_in", [4, P])
    cc_out = place(a, "cc_out", [4, P])
    tail = place(a, "tail", [4, 27])
    silu = place(a, "silu", [4, CV])
    th = place(a, "th", [4, CV])
    gate = place(a, "gate", [2, T])
    samp = place(a, "samp", [3, P])
    k_tok = place(a, "k_tok", [3, P])
    k_t = place(a, "k_t", [3, P])
    qk_r = place(a, "qk_r", [3, P])
    vb = place(a, "vb", [5, P])
    dec = place(a, "dec", [5, P])
    lmat = place(a, "lmat", [5, P])
    xm = place(a, "xm", [5, P])
    ym = place(a, "ym", [5, P])
    p1 = place(a, "p1", [5, P])
    amat = place(a, "amat", [5, P])
    a_t = place(a, "a_t", [5, P])
    k_m = place(a, "k_m", [NSEQ, P])
    s_s = place(a, "s_s", [NSEQ, 2, P])
    s_p = place(a, "s_p", [2, P])
    ud_s = place(a, "ud_s", [2, P])
    ud = place(a, "ud", [2, P])
    u_m = place(a, "u_m", [3, P])
    kq_in = place(a, "kq_in", [2, NSEQ * SLEN])
    ksqs = place(a, "ksqs", [2, P])
    o_m = amat
    cur = place(a, "cur", [50])
    cwcur = place(a, "cwcur", [4, TAPS])
    g = [shared]
    ht = place(g, "ht", [KT, T])
    xtok = place(g, "xtok", [3, DM])
    sq = place(g, "sq", [4, T])
    rb = place(g, "rb", [T])
    vrow = place(g, "vrow", [P])
    crow = place(g, "crow", [2, P])
    lv = place(g, "lv", [LEVELS, P])
    tri_p = place(g, "tri_p", [P])
    tri_s = place(g, "tri_s", [P])
    blk_s = place(g, "blk_s", [P])
    shift = place(g, "shift", [P])
    graw = place(g, "graw", [3, 64])
    gtail = place(g, "gtail", [64])
    gvec = place(g, "gvec", [2, 32])
    gt = place(g, "gt", [3, 32])
    gy = place(g, "gy", [3, 32])
    ge = place(g, "ge", [3, 32])
    gg = place(g, "gg", [3, 32])
    gcs = place(g, "gcs", [3, 32])
    gsb = place(g, "gsb", [NSEQ, 32])
    gct = place(g, "gct", [80])
    gcr = place(g, "gcr", [P])
    c = [shared + KT * T * 4]
    sqp = place(c, "sqp", [2, 2, T])
    rb2 = place(c, "rb2", [T])
    xn = place(c, "xn", [4, T])
    ytok = place(c, "ytok", [3, DM])
    w = [shared + KT * T * 4]
    phi = place(w, "phi", [8, T], F32R)
    plo = place(w, "plo", [8, T], F32R)
    s2z = place(w, "s2z", [8, T])
    ubuf = place(w, "ubuf", [2, PW])
    ws_a = place(w, "ws_a", [2, PW])
    ws_b = place(w, "ws_b", [2, PW])
    pooled = place(w, "pooled", [2, T])
    ztanh = place(w, "ztanh", [2, T])
    cp_in = place(w, "cp_in", [256])
    cp_out = place(w, "cp_out", [256])
    ptail = place(w, "ptail", [2, 79])
    rcount = place(w, "rcount", [NG, PB + 1])
    assert max(a[0], g[0], c[0], w[0]) <= nc.sbuf_usable_end

    ps = nc.alloc_psum_tensor("ps", [P, 8, 512], F32)
    D0, D1, D2, D3 = (ps[:, n, :] for n in (4, 5, 6, 7))
    ht_dram = nc.dram_tensor("ht_save", (P, KT * T), F32, kind="Internal").ap()
    gc_dram = nc.dram_tensor("gc_rows", (NH * 5, P), F32, kind="Internal").ap()

    sems = {}

    def E(name):
        if name not in sems:
            sems[name] = nc.alloc_semaphore(name)
        return sems[name]

    w_in = delta_w_in[0].rearrange("(k p) c -> p k c", p=P)
    w_out = delta_w_out[0].rearrange("(k p) c -> p k c", p=P)
    pw_in = pool_w_in[0].rearrange("(k p) c -> p k c", p=P)
    pw_out = pool_w_out[0].rearrange("(k p) c -> p k c", p=P)
    ENG = ("pe", "act", "dve", "pool")

    def rounds(eng, n):
        for e in ENG:
            eng.wait_ge(E(f"{e}_round"), n)

    def blocks(v, n):
        return v.rearrange("p (u c) -> p u c", u=n)

    def wide(v, n):
        return v.rearrange("p (u o) -> p u o", o=1).to_broadcast([P, n, P])

    def conv_strips(t, n0, n1, skip, take):
        v = t[:, n0:n1, S_AT:].rearrange("p n (b s) -> p n b s", s=SW)
        return v[:, :, :, skip:skip + take]

    def sample_cols(n0, n1):
        return silu[:, n0:n1, NPT:CV].rearrange("p n (b s) -> p n b s", s=SW)[:, :, :, TAPS - 1:]

    def toks(v):
        return v.rearrange("p n (b s) -> p n b s", s=SLEN)

    def pool_strips(t, skip, take):
        return t[:, :, PS_AT:].rearrange("p n (b s) -> p n b s", s=PSW)[:, :, :, skip:skip + take]

    def load(sp, n, slot, halves):
        if not (isinstance(n, int) and n < 4):
            sp.wait_ge(E("w_hi"), n - 3)
            sp.wait_ge(E("w_lo"), n - 3)
        for dst, src in halves:
            sp.dma_start(dst, src).then_inc(E(f"w_landed{slot}"), 16)

    def one_block(slot, w3, k0, c1):
        dst = wraw[:, slot, :].rearrange("p (k c) -> p k c", k=PK)
        return ((dst[:, 0:2, :], w3[:, k0:k0 + 2, bass.ds(c1, 256)]),
                (dst[:, 2:4, :], w3[:, k0 + 2:k0 + 4, bass.ds(c1, 256)]))

    def split_hi(act, n, slot, width=1024):
        act.wait_ge(E(f"w_landed{slot}"), (n - slot) * 8 + 32)
        if not (isinstance(n, int) and n < 4):
            act.wait_ge(E("w_used"), n - 3)
        nc.scalar.activation(whi[:, slot, 0:width], wraw[:, slot, 0:width], ACT.Copy).then_inc(E("w_hi"), 1)

    def split_lo(dve, n, slot, width=1024):
        dve.wait_ge(E("w_hi"), n + 1)
        nc.vector.tensor_tensor(wlo[:, slot, 0:width], wraw[:, slot, 0:width], whi[:, slot, 0:width].bitcast(F32),
                                ALU.subtract).then_inc(E("w_lo"), 1)

    def k_tile(slot, k_w, hi, lo, k_x, pair, first, last):
        mm = nc.tensor.matmul
        for h in range(2):
            w = slice(256 * k_w + P * h, 256 * k_w + P * h + P)
            o = ps[:, 2 * pair + h, 0:T]
            mm(o, whi[:, slot, w], hi[:, k_x, :], start=first, stop=False)
            mm(o, whi[:, slot, w], lo[:, k_x, :], start=False, stop=False)
            done = mm(o, wlo[:, slot, w], hi[:, k_x, :], start=False, stop=last)
        return done

    sq_tok = th[:].rearrange("p n c -> p (n c)")[:, 0:768].rearrange("p (m c) -> p m c", m=2)

    with nc.Block() as block:
        @block.sync
        def _(sp):
            def two_blocks(slot, k0, c1, c2):
                dst = wraw[:, slot, :].rearrange("p (k c) -> p k c", k=PK)
                return ((dst[:, :, 0:P], w_in[:, k0:k0 + PK, bass.ds(c1, P)]),
                        (dst[:, :, P:2 * P], w_in[:, k0:k0 + PK, bass.ds(c2, P)]))

            sp.dma_start(xtok[:, 0, :], x_prompt[0, 0:P, :]).then_inc(E("x_in"), 16)
            sp.dma_start(xtok[:, 1, :], x_prompt[0, P:2 * P, :]).then_inc(E("x_in"), 16)
            sp.dma_start(xtok[0:64, 2, :], x_sample.rearrange("b s c -> (b s) c")).then_inc(E("x_in"), 16)
            for src, r, n in ((norm_w.rearrange("n (k c) -> (n k) c", c=P), 0, 32),
                              (final_norm_w.rearrange("(k c) -> k c", c=P), 32, 16),
                              (pool_scale[0].rearrange("(k c) -> k c", c=P), 48, 32), (delta_o_norm_w, 80, 1)):
                sp.dma_start(vrow[r:r + n, :], src).then_inc(E("rows_in"), 16)
            for h in range(2):
                sp.dma_start(crow[:, h, :], delta_conv_w[0, 2 * h:2 * h + 2, :].rearrange(
                    "j (n c) -> (j n) c", c=P)).then_inc(E("rows_in"), 16)
            sp.dma_start(gvec[:, 0, :], delta_a_log[0].partition_broadcast(P)).then_inc(E("gvec_in"), 16)
            sp.dma_start(gvec[:, 1, :], delta_dt_bias[0].partition_broadcast(P)).then_inc(E("gvec_in"), 16)
            for j in range(4):
                dst = wraw[:, j, 0:256].rearrange("p (k c) -> p k c", k=PK)
                src = w_in[:, PK * j:PK * j + PK, QKV + DI:QKV + DI + 64]
                load(sp, j, j, ((dst[:, 0:2, :], src[:, 0:2, :]), (dst[:, 2:4, :], src[:, 2:4, :])))

            def cache_rows(i):
                cc = cache_conv[0].rearrange("b r c -> (b r) c")
                for n0, n1, c0 in ((0, 1, i * P), (1, 2, i * P + DM), (2, 4, i * 256 + 2 * DM)):
                    sp.dma_start(cc_in[0:24, n0:n1, :].rearrange("p n c -> p (n c)"), cc[:, bass.ds(c0, (n1 - n0) * P)]
                                 ).then_inc(E("cc_landed"), 16)

            def head_weights(i, n):
                for j in range(4):
                    load(sp, n + j, j, two_blocks(j, PK * j, i * P, i * P + DM))
                for j in range(4):
                    load(sp, n + (4 + j), j, one_block(j, w_in, PK * j, i * 256 + 2 * DM))
                if isinstance(i, int):
                    sp.wait_ge(E("x_lo"), KT)
                    sp.wait_ge(E("ht_saved"), 16)
                    cache_rows(i)
                for j in range(4):
                    load(sp, n + (8 + j), j, one_block(j, w_in, PK * j, i * 256 + QKV))

            head_weights(0, HEADS)
            with sp.Fori(1, NH) as i:
                sp.wait_ge(E("cc_t"), i)
                cache_rows(i)
                head_weights(i, i * 12 + HEADS)

            for j in range(4):
                load(sp, OUT_A + j, j, one_block(j, w_out, PK * j, 0))

        @block.gpsimd
        def _(pool):
            gp = nc.gpsimd
            for t in (ident, mask_p, tri_p, blk_s):
                gp.memset(t[:], 0.0 if t in (ident, mask_p) else 1.0).then_inc(E("consts"), 1)
            gp.memset(ones[:], 1.0).then_inc(E("consts"), 1)
            gp.memset(minushalf[:], -0.5).then_inc(E("consts"), 1)
            gp.memset(lv[:], 1.0).then_inc(E("consts"), 1)
            gp.memset(seqmask[:], 1.0).then_inc(E("consts"), 1)
            pool.wait_ge(E("consts"), 8)

            def keep_where(out, in_, base, pattern, cm, fill, op=ALU.is_ge):
                return gp.affine_select(out=out, in_=in_, compare_op=op, fill=fill, base=base, pattern=pattern,
                                        channel_multiplier=cm)

            NB = P // SLEN
            keep_where(ident[:], ident[:], 0, [[-1, P]], 1, 1.0, ALU.not_equal).then_inc(E("ident"), 1)
            keep_where(tri_p[:], tri_p[:], 0, [[1, P]], -1, 0.0).then_inc(E("consts"), 1)
            keep_where(blk_s[:], blk_s[:], 0, [[-SLEN, NB], [0, SLEN]], 1, 0.0).then_inc(E("consts"), 1)
            keep_where(mask_p[:], mask_p[:], 0, [[-1, P]], 1, NEG).then_inc(E("consts"), 1)
            pool.wait_ge(E("consts"), 11)
            keep_where(mask_s[:], mask_p[:], SLEN - 1, [[SLEN, NB], [0, SLEN]], -1, NEG).then_inc(E("consts"), 1)
            keep_where(tri_s[:], tri_p[:], 0, [[-SLEN, NB], [0, SLEN]], 1, 0.0).then_inc(E("consts"), 1)
            keep_where(blk_s[:], blk_s[:], SLEN - 1, [[SLEN, NB], [0, SLEN]], -1, 0.0).then_inc(E("consts"), 1)
            pool.wait_ge(E("ident"), 1)
            for h in range(2):
                gp.tensor_copy(shift[:, 64 * h:64 * h + 64], ident[:, 64:P]).then_inc(E("consts"), 1)
            pool.wait_ge(E("consts"), 16)
            for step, (base, pattern, cm) in enumerate(((0, [[-SLEN, NSEQ]], 1), (SLEN - 1, [[SLEN, NSEQ]], -1))):
                for h in range(2):
                    v = seqmask[64 * h:64 * h + 64, :]
                    keep_where(v, v, base, pattern, cm, 0.0).then_inc(E("consts"), 1)
                    pool.wait_ge(E("consts"), 16 + 2 * step + h + 1)
            for step in range(3):
                for k in range(LEVELS):
                    b = 1 << k
                    v = lv[:, k, :].rearrange("p (j r) -> p j r", r=2 * b)
                    n = P // (2 * b)
                    base, pattern, cm = ((-b, [[-2 * b, n], [0, 2 * b]], 1), (2 * b - 1, [[2 * b, n], [0, 2 * b]], -1),
                                         (b - 1, [[0, n], [-1, 2 * b]], 0))[step]
                    keep_where(v, v, base, pattern, cm, 0.0).then_inc(E("consts"), 1)
                pool.wait_ge(E("consts"), 20 + LEVELS * (step + 1))
            gp.tensor_copy(level[:], lv[:]).then_inc(E("c_all"), 1)
            pool.wait_ge(E("x_lo"), KT)
            pool.wait_ge(E("ht_saved"), 16)
            gp.memset(convin[:, :, 0:TAPS - 1], 0.0).then_inc(E("conv_zero"), 1)
            for e in ("pe", "act", "dve"):
                pool.wait_ge(E(f"{e}_round"), 1)
            gp.memset(ud_s[:], 0.0)
            gp.memset(small[:], 0.0).then_inc(E("pool_round"), 1)

            def delta(n):
                rounds(pool, n)
                pool.wait_ge(E("ident"), 1)
                for u in range(5):
                    last = gp.tensor_tensor(xm[:, u, :], ident[:], ones[:], ALU.mult)
                last.then_inc(E("x_init"), 1)
                pool.wait_ge(E("sum_sb"), n)
                gp.tensor_tensor(small[:, 8:14], small[:, 0:6], minushalf[:, 0:6], ALU.pow).then_inc(E("rnorm"), 1)
                pool.wait_ge(E("rnorm"), n)
                pool.wait_ge(E("cur"), n)
                gp.tensor_tensor(small[:, 16:20].rearrange("p (v c) -> p v c", v=2),
                                 small[:, 8:10].rearrange("p (o c) -> p o c", o=1).to_broadcast([P, 2, 2]),
                                 cur[:, EGC:EGC + 4].rearrange("p (v c) -> p v c", v=2), ALU.mult)
                gp.tensor_tensor(small[:, 20:21], small[:, 10:11], cur[:, EGC + 4:EGC + 5], ALU.mult).then_inc(E("rqe"), 1)
                pool.wait_ge(E("dec"), n)
                pool.wait_ge(E("qk_r"), n)
                for v in range(2):
                    gp.tensor_tensor(amat[:, 2 * v:2 * v + 2, :], qk_r[:, 0:2, :], dec[:, 2 * v:2 * v + 2, :], ALU.mult)
                gp.tensor_tensor(amat[:, 4, :], qk_r[:, 2, :], dec[:, 4, :], ALU.mult).then_inc(E("a_mat"), 1)
                pool.wait_ge(E("k_tok"), n)
                gp.tensor_tensor(k_m[:], k_tok[:, 2:3, :].to_broadcast([P, NSEQ, P]), wide(seqmask[:], NSEQ), ALU.mult
                                 ).then_inc(E("k_m"), 1)
                pool.wait_ge(E("ksqs_ps"), n)
                sv = s_s[:].rearrange("p b v c -> p (b v) c")
                gp.tensor_tensor(sv, sv, wide(cur[:, EGL + 4:EGL + 20], 16), ALU.mult).then_inc(E("s_scaled"), 1)
                pool.wait_ge(E("osum_sb"), n)
                gp.tensor_tensor(small[:, 32:37], small[:, 24:29], minushalf[:, 0:5], ALU.pow).then_inc(E("ro"), 1)
                pool.wait_ge(E("ro"), n)
                gp.tensor_tensor(small[:, 40:41], ones[:, 0:1], ones[:, 0:1], ALU.mult).then_inc(E("pool_round"), 1)

            with pool.Fori(1, NH) as i:
                delta(i)
            delta(NH)

        @block.scalar
        def _(act):
            sc = nc.scalar

            for k in range(0, KT, 2):
                act.wait_ge(E("tiles_t"), k + 1)
                sc.activation(ht[:, k, :], ps[:, 4 + k % 4, 0:T], ACT.Copy).then_inc(E("even_tiles"), 1)
                if k >= 4:
                    act.wait_ge(E("sq_used"), k - 3)
                act.wait_ge(E("even_tiles"), k // 2 + 1)
                sc.activation(sq[:, k % 4, :], ht[:, k, :], ACT.Square).then_inc(E("sq_even"), 1)
            act.wait_ge(E("odd_tiles"), KT // 2)
            act.dma_start(ht_dram, ht[:].rearrange("p k t -> p (k t)")).then_inc(E("ht_saved"), 16)
            act.wait_ge(E("ms"), 1)
            sc.activation(rb[:], rb[:], ACT.Sqrt).then_inc(E("rms"), 1)
            for n in range(4):
                split_hi(act, n, n, 256)
            for k in range(KT):
                act.wait_ge(E("xnorm"), k + 1)
                sc.activation(xhi[:, k, :], sq[:, k % 4, :], ACT.Copy).then_inc(E("x_hi"), 1)
            split_hi(act, HEADS, 0)
            split_hi(act, HEADS + 1, 1)
            act.wait_ge(E("gvec_in"), 32)
            sc.activation(gvec[:, 0, :], gvec[:, 0, :], ACT.Exp).then_inc(E("g_act"), 1)
            act.wait_ge(E("graw"), 1)
            sc.activation(gt[:], graw[:, :, 0:32], ACT.Tanh, scale=0.5).then_inc(E("g_act"), 1)
            act.wait_ge(E("gy"), 1)
            sc.activation(ge[:], gy[:], ACT.Abs).then_inc(E("g_act"), 1)
            act.wait_ge(E("g_act"), 3)
            sc.activation(ge[:], ge[:], ACT.Exp, scale=-1.0).then_inc(E("g_act"), 1)
            act.wait_ge(E("g_act"), 4)
            sc.activation(ge[:], ge[:], ACT.Ln, bias=1.0).then_inc(E("g_act"), 1)
            split_hi(act, HEADS + 2, 2)
            split_hi(act, HEADS + 3, 3)
            split_hi(act, HEADS + 4, 0)
            split_hi(act, HEADS + 5, 1)
            act.wait_ge(E("t_raw"), 1)
            tv = table[:, :, 0:30].rearrange("p h (t u) -> p h t u", u=5)
            sc.activation(tv[:, :, 4, :], tv[:, :, 0, :], ACT.Exp)
            sc.activation(tv[:, :, 5, :], tv[:, :, 5, :], ACT.Exp)
            sc.activation(table[:, :, EGL:EGL + 20], table[:, :, EGL:EGL + 20], ACT.Exp).then_inc(E("t_exp"), 1)
            act.wait_ge(E("gcr"), 1)
            act.dma_start(gc_dram, gcr[0:80, :]).then_inc(E("delta_out"), 16)

            def loop_of(i):
                return not isinstance(i, int)

            def qk_evac(i, used):
                act.wait_ge(E("w_used"), used)
                if loop_of(i):
                    act.wait_ge(E("conv"), i * 16)
                sc.activation(convin[:, 0:2, TAPS - 1:S_AT], ps[:, 0:2, 0:NPT], ACT.Copy)
                sc.activation(conv_strips(convin, 0, 2, TAPS - 1, SLEN), toks(ps[:, 0:2, NPT:T]), ACT.Copy
                              ).then_inc(E("qk_evac"), 1)

            def v_evac(i, used):
                act.wait_ge(E("w_used"), used)
                if loop_of(i):
                    act.wait_ge(E("conv"), i * 16)
                sc.activation(convin[:, 2:4, TAPS - 1:S_AT], ps[:, 2:4, 0:NPT], ACT.Copy)
                sc.activation(conv_strips(convin, 2, 4, TAPS - 1, SLEN), toks(ps[:, 2:4, NPT:T]), ACT.Copy
                              ).then_inc(E("v_evac"), 1)

            def z_evac(i, used):
                act.wait_ge(E("w_used"), used)
                if loop_of(i):
                    act.wait_ge(E("gate"), i)
                sc.activation(zraw[:], ps[:, 0:2, 0:T], ACT.Copy).then_inc(E("z_evac"), 1)

            def cc_evac(i):
                if loop_of(i):
                    act.wait_ge(E("conv"), i * 16)
                act.wait_ge(E("cc_t"), i + 1)
                sc.activation(conv_strips(convin, 0, 4, 0, TAPS - 1),
                              D3[:, 0:96].rearrange("p (n b r) -> p n b r", n=4, b=NSEQ), ACT.Copy
                              ).then_inc(E("cc_evac"), 1)

            def cc_tail(i):
                if loop_of(i):
                    act.wait_ge(E("cc_o"), i)
                act.wait_ge(E("qk_evac"), i + 1)
                act.wait_ge(E("v_evac"), i + 1)
                sc.activation(tail[:, :, 0:24].rearrange("p n (b r) -> p n b r", b=NSEQ),
                              conv_strips(convin, 0, 4, SLEN, TAPS - 1), ACT.Copy)
                sc.activation(tail[:, :, 24:27], convin[:, :, NPT:NPT + 3], ACT.Copy).then_inc(E("tail"), 1)

            def cc_store(i):
                if loop_of(i):
                    act.wait_ge(E("cc_dma"), i * 96)
                act.wait_ge(E("cc_o"), i + 1)
                sc.activation(cc_out[0:27, :, :], blocks(D3[0:27, :], 4), ACT.Copy).then_inc(E("cc_out"), 1)
                act.wait_ge(E("cc_out"), i + 1)
                s_rows, p_rows = new_cc_s[0].rearrange("b r c -> (b r) c"), new_cc_p[0, 0]
                for n0, n1, c0 in ((0, 1, i * P), (1, 2, i * P + DM), (2, 4, i * 256 + 2 * DM)):
                    v = cc_out[:, n0:n1, :].rearrange("p n c -> p (n c)")
                    act.dma_start(s_rows[:, bass.ds(c0, (n1 - n0) * P)], v[0:24, :]).then_inc(E("cc_dma"), 16)
                    act.dma_start(p_rows[:, bass.ds(c0, (n1 - n0) * P)], v[24:27, :]).then_inc(E("cc_dma"), 16)

            def copy_units(dst, name, samples):
                last = sc.activation(dst[:, 0:4, :], blocks(D0, 4), ACT.Copy)
                if samples:
                    last = sc.activation(dst[:, 4, :], D1[:, 0:P], ACT.Copy)
                last.then_inc(E(name), 1)

            def delta(n, d, split, cached):
                act.wait_ge(E("delta_out"), 16)
                rounds(act, n)
                act.dma_start(dec[:].rearrange("p u c -> p (u c)"),
                              gc_dram.rearrange("r c -> (r c)")[bass.ds(d * (5 * P), 5 * P)].partition_broadcast(P)
                              ).then_inc(E("dec_landed"), 16)
                split(0)
                act.wait_ge(E("conv"), n * 16 - 2)
                sc.activation(th[:, 0:2, :], silu[:, 0:2, :], ACT.Tanh, scale=0.5).then_inc(E("th_qk"), 1)
                act.wait_ge(E("conv"), n * 16)
                sc.activation(th[:, 2:4, :], silu[:, 2:4, :], ACT.Tanh, scale=0.5).then_inc(E("th_v"), 1)
                act.wait_ge(E("diff"), n)
                sc.activation(dec[:], dec[:], ACT.Exp).then_inc(E("dec"), 1)
                split(1)
                if loop_of(n):
                    act.wait_ge(E("delta_out"), n * 48 - 32)
                elif n > 1:
                    act.wait_ge(E("delta_out"), 48 * n - 32)
                sd = state_delta[0].rearrange("b h d e -> d h b e")
                for v in range(2):
                    act.dma_start(s_s[:, :, v, :], sd[:, bass.ds(d * 2 + v, 1), :, :].rearrange("d h b e -> d (h b) e")
                                  ).then_inc(E("state_landed"), 16)
                act.wait_ge(E("silu"), n)
                for q in range(2):
                    sc.activation(samp[:, q, :].rearrange("p (o b s) -> p o b s", o=2, b=NSEQ),
                                  sample_cols(q, q + 1).to_broadcast([P, 2, NSEQ, SLEN]), ACT.Copy)
                sc.activation(samp[:, 2, :].rearrange("p (o b s) -> p o b s", o=2, b=NSEQ), sample_cols(2, 4), ACT.Copy
                              ).then_inc(E("samp"), 1)
                act.wait_ge(E("samp"), n)
                sc.activation(sq_tok[:, :, 0:NPT], silu[:, 0:2, 0:NPT], ACT.Square)
                sc.activation(sq_tok[:, :, NPT:384], samp[:, 0:2, :], ACT.Square).then_inc(E("qk_sq"), 1)
                act.wait_ge(E("z_evac"), n)
                sc.activation(gate[:], zraw[:], ACT.Tanh, scale=0.5).then_inc(E("z_tanh"), 1)
                split(2)
                act.wait_ge(E("kn_ps"), n)
                sc.activation(k_t[:], blocks(D3[:, 0:384], 3), ACT.Copy)
                sc.activation(kq_in[:, 0, :], D3[:, 256:320], ACT.Copy)
                sc.activation(kq_in[:, 1, :], samp[:, 0, 0:64], ACT.Copy).then_inc(E("k_t"), 1)
                split(3)
                act.wait_ge(E("xt"), (n - 1) * LEVELS + 1)
                copy_units(ym, "y", True)
                act.wait_ge(E("at_ps"), n)
                sc.activation(a_t[:, 0:4, :], blocks(D2, 4), ACT.Copy)
                sc.activation(a_t[:, 4, :], D3[:, 0:P], ACT.Copy).then_inc(E("a_t"), 1)
                for k in range(1, LEVELS):
                    act.wait_ge(E("lp"), (n - 1) * (LEVELS - 1) + k)
                    copy_units(p1, "p", k < S_LEVELS)
                    if k == 6:
                        cached()
                    if k != 3:
                        split({1: 4, 2: 5, 4: 6, 5: 7, 6: 8}[k])
                    act.wait_ge(E("xt"), (n - 1) * LEVELS + (k + 1))
                    copy_units(ym, "y", k < S_LEVELS)
                    if k == 3:
                        act.wait_ge(E("ksqs_ps"), n)
                        sc.activation(ksqs[:], blocks(D3[:, 0:256], 2), ACT.Copy).then_inc(E("ksqs"), 1)
                act.wait_ge(E("u0_ps"), n)
                sc.activation(u_m[:], blocks(D1[:, 0:384], 3), ACT.Copy).then_inc(E("u0"), 1)
                act.wait_ge(E("s0_ps"), n)
                sc.activation(s_p[:], blocks(D0[:, 0:256], 2), ACT.Copy).then_inc(E("s0"), 1)
                split(9)
                act.wait_ge(E("u1_ps"), n)
                sc.activation(u_m[:, 0:2, :], blocks(D2[:, 0:256], 2), ACT.Copy).then_inc(E("u1"), 1)
                split(10)
                act.wait_ge(E("o_all"), n)
                for u in range(5):
                    sc.activation(p1[:, u, :], o_m[:, u, :], ACT.Square, accum_out=small[:, 48 + u:49 + u]
                                  ).then_inc(E("osq"), 1)
                act.wait_ge(E("sp_final"), n)
                act.dma_start(new_sd_p[0, 0].rearrange("h d e -> d h e")[:, bass.ds(d * 2, 2), :], s_p[:]
                              ).then_inc(E("delta_out"), 16)
                act.wait_ge(E("ss_sum"), n * 4)
                sdo = new_sd_s[0].rearrange("b h d e -> d h b e")
                for v in range(2):
                    act.dma_start(sdo[:, bass.ds(d * 2 + v, 1), :, :].rearrange("d h b e -> d (h b) e"), s_s[:, :, v, :]
                                  ).then_inc(E("delta_out"), 16)
                split(11)
                act.wait_ge(E("osq"), n * 5)
                sc.activation(small[:, 60:61], ones[:, 0:1], ACT.Copy).then_inc(E("act_round"), 1)

            act.wait_ge(E("x_lo"), KT)
            act.wait_ge(E("ht_saved"), 16)
            act.wait_ge(E("conv_zero"), 1)
            qk_evac(0, HEADS + 4)
            cc_evac(0)
            for j in range(6, 10):
                split_hi(act, HEADS + j, j % 4)
            v_evac(0, HEADS + 8)
            cc_tail(0)
            cc_store(0)
            for j in range(10, 12 + LEAD):
                split_hi(act, HEADS + j, j % 4)
            z_evac(0, HEADS + 12)
            act.wait_ge(E("t_exp"), 1)
            sc.activation(cwcur[:, 0, 0:1], ones[:, 0:1], ACT.Copy).then_inc(E("act_round"), 1)

            with act.Fori(1, NH) as i:
                def split(j, i=i):
                    split_hi(act, i * 12 + (HEADS + LEAD + j), (LEAD + j) % 4)
                    if j == 3:
                        qk_evac(i, i * 12 + (HEADS + 4))
                    if j == 8:
                        v_evac(i, i * 12 + (HEADS + 8))
                        cc_tail(i)
                    if j == 10:
                        cc_store(i)

                delta(i, i - 1, split, lambda i=i: cc_evac(i))
                z_evac(i, i * 12 + (HEADS + 12))
            delta(NH, NH - 1, lambda j: None, lambda: None)


        @block.vector
        def _(dve):
            v = nc.vector

            for k in range(1, KT, 2):
                dve.wait_ge(E("tiles_t"), k + 1)
                v.tensor_copy(ht[:, k, :], ps[:, 4 + k % 4, 0:T]).then_inc(E("odd_tiles"), 1)
                if k >= 4:
                    dve.wait_ge(E("sq_used"), k - 3)
                dve.wait_ge(E("odd_tiles"), k // 2 + 1)
                v.tensor_tensor(sq[:, k % 4, :], ht[:, k, :], ht[:, k, :], ALU.mult).then_inc(E("sq_odd"), 1)
            dve.wait_ge(E("vecs_ps"), 1)
            v.tensor_copy(vecs[:, 0:V_SCALE], ps[:, 1, 0:V_SCALE])
            v.tensor_scalar(vecs[:, V_SCALE:V_O + 1], ps[:, 1, V_SCALE:V_O + 1], 0.5, None, ALU.mult).then_inc(E("vecs"), 1)
            cw = ps[:, 2, 0:256].rearrange("p (t n) -> p t n", t=TAPS)
            for q in range(2):
                v.tensor_copy(convw[:, :, q, :].rearrange("p h t -> p t h"), cw[:, :, NH * q:NH * q + NH])
            for q in range(2):
                last = v.tensor_copy(convw[:, :, 2 + q, :].rearrange("p h t -> p t h"),
                                     cw[:, :, 2 * NH:4 * NH].rearrange("p t (h v) -> p t h v", v=2)[:, :, :, q])
            last.then_inc(E("convw"), 1)
            dve.wait_ge(E("sq_used"), KT)
            v.tensor_scalar(rb[:], ps[:, 0, 0:T], 1.0 / DM, EPS, ALU.mult, ALU.add).then_inc(E("ms"), 1)
            dve.wait_ge(E("rms"), 1)
            v.reciprocal(rb[:], rb[:]).then_inc(E("rinv"), 1)
            dve.wait_ge(E("rinv"), 1)
            dve.wait_ge(E("vecs"), 1)

            def low_x(k):
                dve.wait_ge(E("x_hi"), k + 1)
                v.tensor_tensor(xlo[:, k, :], sq[:, k % 4, :], xhi[:, k, :].bitcast(F32), ALU.subtract
                                ).then_inc(E("x_lo"), 1)

            for k in range(KT):
                if k >= 4:
                    dve.wait_ge(E("x_lo"), k - 3)
                v.scalar_tensor_tensor(sq[:, k % 4, :], ht[:, k, :], vecs[:, k:k + 1], rb[:], ALU.mult, ALU.mult
                                       ).then_inc(E("xnorm"), 1)
                if k == 1:
                    for n in range(4):
                        split_lo(dve, n, n, 256)
                if k >= 1:
                    low_x(k - 1)
            low_x(KT - 1)
            split_lo(dve, HEADS, 0)
            split_lo(dve, HEADS + 1, 1)

            dve.wait_ge(E("w_used"), 4)
            v.tensor_copy(graw[:, 0:2, :], blocks(D0[:, 0:128], 2))
            v.tensor_copy(gtail[:], D0[:, 128:192]).then_inc(E("gtail"), 1)
            dve.wait_ge(E("g_pe"), 1)
            v.tensor_copy(graw[:, 2, :], D1[:, 0:64]).then_inc(E("graw"), 1)
            dve.wait_ge(E("graw"), 1)
            dve.wait_ge(E("gvec_in"), 32)
            v.tensor_tensor(gy[:], graw[:, :, 32:64], gvec[:, 1:2, :].to_broadcast([P, 3, 32]), ALU.add).then_inc(E("gy"), 1)
            split_lo(dve, HEADS + 2, 2)
            split_lo(dve, HEADS + 3, 3)
            dve.wait_ge(E("g_act"), 2)
            def put(col0, src):
                v.tensor_copy(table[:, :, col0:col0 + 4].rearrange("p h (v c) -> p h v c", v=2),
                              src[:, 0:2, :].rearrange("p c (h v) -> p h v c", v=2))
                for q in range(2):
                    last = v.tensor_copy(table[64 * q:64 * q + 64, :, col0 + 4],
                                         src[64 * q:64 * q + 64, 2, :].rearrange("p (h v) -> p h v", v=2)[:, :, q])
                return last

            dve.wait_ge(E("g_act"), 5)
            v.scalar_tensor_tensor(gg[:], gy[:], 0.0, ge[:], ALU.max, ALU.add).then_inc(E("g_vec"), 1)
            dve.wait_ge(E("g_vec"), 1)
            v.scalar_tensor_tensor(gg[:], gg[:], -1.0, gvec[:, 0:1, :].to_broadcast([P, 3, 32]), ALU.mult, ALU.mult
                                   ).then_inc(E("g_vec"), 1)
            dve.wait_ge(E("g_vec"), 2)
            dve.wait_ge(E("consts"), 20)
            v.tensor_tensor(gsb[0:64, :, :], gg[0:64, 2:3, :].to_broadcast([64, NSEQ, 32]),
                            seqmask[0:64, :].rearrange("p (b o) -> p b o", o=1).to_broadcast([64, NSEQ, 32]), ALU.mult
                            ).then_inc(E("gg"), 1)
            split_lo(dve, HEADS + 4, 0)
            split_lo(dve, HEADS + 5, 1)
            v.tensor_scalar(gy[:], gt[:], -0.5, -0.5, ALU.mult, ALU.add)
            v.tensor_scalar(ge[:], gt[:], 0.25, 0.25, ALU.mult, ALU.add).then_inc(E("g_vec"), 1)
            dve.wait_ge(E("g_vec"), 3)
            put(NBETA, gy)
            put(HBETA, ge)
            dve.wait_ge(E("g_pe"), 2)
            gc3, gl3 = blocks(D2[:, 0:96], 3), blocks(D2[:, 96:192], 3)
            v.tensor_copy(gcs[:], gc3).then_inc(E("g_vec"), 1)
            dve.wait_ge(E("g_vec"), 4)
            v.tensor_tensor(gt[:], gl3, gcs[:], ALU.subtract).then_inc(E("g_vec"), 1)
            put(GC, gcs)
            v.tensor_copy(table[:, :, EGL:EGL + 4].rearrange("p h (c v) -> p h c v", v=2),
                          gl3[:, 0:2, :].rearrange("p c (h v) -> p h c v", v=2))
            v.tensor_copy(table[:, :, EGL + 4:EGL + 20].rearrange("p h (b v) -> p h b v", v=2),
                          D3[:, 0:256].rearrange("p (b h v) -> p h b v", b=NSEQ, v=2))
            dve.wait_ge(E("g_vec"), 5)
            put(DEC, gt).then_inc(E("t_raw"), 1)
            dve.wait_ge(E("t_raw"), 1)
            v.tensor_scalar(blocks(gct[:], NH), table[:, :, GC:GC + 5], -1.0, None, ALU.mult).then_inc(E("gct"), 1)
            dve.wait_ge(E("g_pe"), 3)
            v.tensor_copy(gcr[0:80, :], D1[0:80, 0:P]).then_inc(E("gcr"), 1)
            dve.wait_ge(E("t_exp"), 1)
            v.tensor_tensor(table[:, :, NBE:NBE + 5], table[:, :, NBETA:NBETA + 5], table[:, :, EGC:EGC + 5], ALU.mult
                            ).then_inc(E("table"), 1)

            def delta(n, d, split):
                rounds(dve, n)
                dve.wait_ge(E("table"), 1)
                v.tensor_copy(cur[:], table[:, bass.ds(d, 1), :].rearrange("p h c -> p (h c)"))
                v.tensor_copy(cwcur[:], convw[:, bass.ds(d, 1), :, :].rearrange("p h q t -> p (h q) t")).then_inc(E("cur"), 1)
                split(0)
                dve.wait_ge(E("cur"), n)
                dve.wait_ge(E("qk_evac"), n)
                dve.wait_ge(E("v_evac"), n)
                dve.wait_ge(E("cc_evac"), n)
                dve.wait_ge(E("conv_zero"), 1)
                for j in range(TAPS):
                    for q in range(4):
                        if j == 0:
                            ins = v.tensor_scalar(silu[:, q, :], convin[:, q, 0:CV], cwcur[:, q, 0:1], None, ALU.mult)
                        else:
                            dve.wait_ge(E("conv"), (n - 1) * 16 + (4 * (j - 1) + q + 1))
                            ins = v.scalar_tensor_tensor(silu[:, q, :], convin[:, q, j:j + CV], cwcur[:, q, j:j + 1],
                                                         silu[:, q, :], ALU.mult, ALU.add)
                        ins.then_inc(E("conv"), 1)
                dve.wait_ge(E("dec_landed"), n * 16)
                for u in range(5):
                    last = v.scalar_tensor_tensor(dec[:, u, :], dec[:, u, :], cur[:, GC + u:GC + u + 1],
                                                  mask_p[:] if u < 4 else mask_s[:], ALU.add, ALU.add)
                last.then_inc(E("diff"), 1)
                split(1)
                dve.wait_ge(E("th_qk"), n)
                v.scalar_tensor_tensor(silu[:, 0:2, :], th[:, 0:2, :], 1.0, silu[:, 0:2, :], ALU.add, ALU.mult)
                dve.wait_ge(E("th_v"), n)
                v.scalar_tensor_tensor(silu[:, 2:4, :], th[:, 2:4, :], 1.0, silu[:, 2:4, :], ALU.add, ALU.mult
                                       ).then_inc(E("silu"), 1)
                dve.wait_ge(E("z_tanh"), n)
                v.scalar_tensor_tensor(gate[:], gate[:], 1.0, zraw[:], ALU.add, ALU.mult).then_inc(E("gate"), 1)
                dve.wait_ge(E("sums_ps"), n)
                v.tensor_scalar(small[:, 0:3], D0[:, 0:3], float(P), 4 * P * EPS, ALU.mult, ALU.add)
                v.tensor_scalar(small[:, 3:6], D0[:, 3:6], 4 * EPS, None, ALU.add).then_inc(E("sum_sb"), 1)
                dve.wait_ge(E("kv_ps"), n)
                v.tensor_tensor(vb[:, 0:4, :], blocks(D2, 4), wide(cur[:, HBETA:HBETA + 4], 4), ALU.mult)
                v.tensor_scalar(vb[:, 4, :], D1[:, 384:512], cur[:, HBETA + 4:HBETA + 5], None, ALU.mult).then_inc(E("vb"), 1)
                split(2)
                dve.wait_ge(E("rnorm"), n)
                v.tensor_tensor(k_tok[:], blocks(D1[:, 0:384], 3), wide(small[:, 11:14], 3), ALU.mult).then_inc(E("k_tok"), 1)
                split(3)
                dve.wait_ge(E("kk_ps"), n)
                dve.wait_ge(E("dec"), n)
                for u in range(5):
                    last = v.scalar_tensor_tensor(lmat[:, u, :], D0[:, P * (u % 2 if u < 4 else 2):P * (u % 2 if u < 4 else 2) + P],
                                                  cur[:, NBETA + u:NBETA + u + 1], dec[:, u, :], ALU.mult, ALU.mult)
                last.then_inc(E("l_mat"), 1)
                dve.wait_ge(E("qk_ps"), n)
                v.tensor_tensor(qk_r[:], blocks(D1[:, 0:384], 3), wide(small[:, 8:11], 3), ALU.mult).then_inc(E("qk_r"), 1)
                dve.wait_ge(E("c_all"), 1)
                dve.wait_ge(E("x_init"), n)
                dve.wait_ge(E("l_mat"), n)
                v.copy_predicated(xm[:], level[:, 0:1, :].to_broadcast([P, 5, P]), lmat[:]).then_inc(E("x"), 1)
                for k in range(1, LEVELS):
                    if k not in (3, 4):
                        split({1: 4, 2: 5, 5: 6, 6: 7}[k])
                    dve.wait_ge(E("c_all"), 1)
                    dve.wait_ge(E(f"lx{k}"), n)
                    last = v.copy_predicated(xm[:, 0:4, :], level[:, k:k + 1, :].to_broadcast([P, 4, P]), blocks(D2, 4))
                    if k < S_LEVELS:
                        last = v.copy_predicated(xm[:, 4, :], level[:, k, :], D3[:, 0:P])
                    last.then_inc(E("x"), 1)
                    if k == 4:
                        dve.wait_ge(E("ksqs_t"), n)
                        dve.wait_ge(E("rqe"), n)
                        v.scalar_tensor_tensor(vb[:, 4, :], D3[:, 256:384], cur[:, NBE + 4:NBE + 5], vb[:, 4, :], ALU.mult, ALU.add
                                               ).then_inc(E("r4"), 1)
                        v.tensor_scalar(o_m[:, 4, :], D3[:, 384:512], small[:, 20:21], None, ALU.mult).then_inc(E("o4"), 1)
                split(8)
                dve.wait_ge(E("u0"), n)
                v.tensor_tensor(ud[:], u_m[:, 0:2, :], wide(cur[:, DEC:DEC + 4:2], 2), ALU.mult).then_inc(E("ud0"), 1)
                for q in range(2):
                    r = slice(64 * q, 64 * q + 64)
                    last = v.tensor_scalar(ud_s[r, q, :], u_m[r, 2, :], cur[r, DEC + 4:DEC + 5], None, ALU.mult)
                last.then_inc(E("ud_s"), 1)
                dve.wait_ge(E("au0_ps"), n)
                dve.wait_ge(E("o4"), n)
                v.tensor_copy(o_m[:, 0:4:2, :], blocks(D2[:, 0:256], 2))
                v.tensor_tensor(o_m[:, 4, :], D2[:, 256:384], o_m[:, 4, :], ALU.add).then_inc(E("o_c0"), 1)
                split(9)
                dve.wait_ge(E("ksqs1"), n)
                for q in range(2):
                    u = 2 * q + 1
                    last = v.scalar_tensor_tensor(vb[:, u, :], D1[:, P * q:P * q + P], cur[:, NBE + u:NBE + u + 1], vb[:, u, :],
                                                  ALU.mult, ALU.add)
                last.then_inc(E("r1"), 1)
                for q in range(2):
                    last = v.tensor_scalar(o_m[:, 2 * q + 1, :], D1[:, 256 + P * q:384 + P * q], small[:, 17 + 2 * q:18 + 2 * q],
                                           None, ALU.mult)
                last.then_inc(E("o1"), 1)
                dve.wait_ge(E("u1"), n)
                dve.wait_ge(E("s0_ps"), n)
                v.tensor_tensor(ud[:], u_m[:, 0:2, :], wide(cur[:, DEC + 1:DEC + 5:2], 2), ALU.mult).then_inc(E("ud1"), 1)
                dve.wait_ge(E("au1_ps"), n)
                dve.wait_ge(E("o1"), n)
                v.tensor_tensor(o_m[:, 1:4:2, :], blocks(D0[:, 0:256], 2), o_m[:, 1:4:2, :], ALU.add).then_inc(E("o_all"), 1)
                dve.wait_ge(E("s1_ps"), n)
                for q in range(2):
                    last = v.scalar_tensor_tensor(s_p[:, q, :], s_p[:, q, :], cur[:, EGL + 2 + q:EGL + 3 + q],
                                                  D1[:, P * q:P * q + P], ALU.mult, ALU.add)
                last.then_inc(E("sp_final"), 1)
                split(10)
                dve.wait_ge(E("osq"), n * 5)
                v.tensor_scalar(small[:, 24:29], small[:, 48:53], 1.0 / P, EPS, ALU.mult, ALU.add).then_inc(E("osum_sb"), 1)
                dve.wait_ge(E("s_scaled"), n)
                for q in range(4):
                    dve.wait_ge(E("ss_ps"), (n - 1) * 4 + (q + 1))
                    w = s_s[:, 2 * q:2 * q + 2, :, :].rearrange("p b v c -> p (b v c)")
                    v.tensor_tensor(w, (D2, D3)[q % 2], w, ALU.add).then_inc(E("ss_sum"), 1)
                split(11)
                dve.wait_ge(E("ro"), n)
                v.tensor_tensor(o_m[:], o_m[:], wide(small[:, 32:37], 5), ALU.mult).then_inc(E("on"), 1)
                dve.wait_ge(E("ot_ps"), n)
                b = branch[:, bass.ds(d * 2, 2), :]
                v.scalar_tensor_tensor(b[:, :, 0:NPT], blocks(D0, 2), vecs[:, V_O:V_O + 1], gate[:, :, 0:NPT], ALU.mult, ALU.mult)
                v.scalar_tensor_tensor(b[:, :, NPT:T], blocks(D1[:, 0:P], 2), vecs[:, V_O:V_O + 1], gate[:, :, NPT:T],
                                       ALU.mult, ALU.mult).then_inc(E("dve_round"), 1)

            for j in range(6, 12 + LEAD):
                split_lo(dve, HEADS + j, j % 4)
            dve.wait_ge(E("table"), 1)
            v.tensor_copy(small[:, 62:63], ones[:, 0:1]).then_inc(E("dve_round"), 1)
            with dve.Fori(1, NH) as i:
                delta(i, i - 1, lambda j, i=i: split_lo(dve, i * 12 + (HEADS + LEAD + j), (LEAD + j) % 4))
            delta(NH, NH - 1, lambda j: None)

        @block.tensor
        def _(pe):
            mm = nc.tensor.matmul
            tr = nc.tensor.transpose

            def one(out, lhsT, rhs):
                return mm(out, lhsT, rhs, start=True, stop=True)

            pe.wait_ge(E("ident"), 1)
            pe.wait_ge(E("x_in"), 48)
            for k in range(KT):
                if k >= 4:
                    pe.wait_ge(E("odd_tiles" if k % 2 else "even_tiles"), (k - 4) // 2 + 1)
                b = ps[:, 4 + k % 4, :]
                tr(b[:, 0:P], xtok[:, 0, P * k:P * k + P], ident[:])
                tr(b[:, P:2 * P], xtok[:, 1, P * k:P * k + P], ident[:])
                tr(b[:, 2 * P:T], xtok[0:64, 2, P * k:P * k + P], ident[0:64, 0:64]).then_inc(E("tiles_t"), 1)
                if k == 3:
                    pe.wait_ge(E("rows_in"), 96)
                    tr(ps[:, 1, 0:V_O + 1], vrow[0:V_O + 1, :], ident[0:V_O + 1, 0:V_O + 1]).then_inc(E("vecs_ps"), 1)
                    for h in range(2):
                        last = tr(ps[:, 2, P * h:P * h + P], crow[:, h, :], ident[:])
                    last.then_inc(E("vecs_ps"), 1)
                if k >= 3:
                    q = k - 3
                    pe.wait_ge(E("sq_odd" if q % 2 else "sq_even"), q // 2 + 1)
                    pe.wait_ge(E("consts"), 8)
                    mm(ps[:, 0, 0:T], ones[:], sq[:, q % 4, :], start=q == 0, stop=False).then_inc(E("sq_used"), 1)
            for q in range(KT - 3, KT):
                pe.wait_ge(E("sq_odd" if q % 2 else "sq_even"), q // 2 + 1)
                mm(ps[:, 0, 0:T], ones[:], sq[:, q % 4, :], start=False, stop=q == KT - 1).then_inc(E("sq_used"), 1)
            for k in range(KT):
                if k % 4 == 0:
                    pe.wait_ge(E("w_lo"), k // 4 + 1)
                pe.wait_ge(E("x_lo"), k + 1)
                for q, c0 in enumerate((0, P, T - P)):
                    w = slice(64 * (k % 4), 64 * (k % 4) + 64)
                    o = D0[:, 64 * q:64 * q + 64]
                    mm(o, xhi[:, k, c0:c0 + P], whi[:, k // 4, w], start=k == 0 and q == 0, stop=False, skip_group_check=True)
                    mm(o, xhi[:, k, c0:c0 + P], wlo[:, k // 4, w], start=False, stop=False, skip_group_check=True)
                    last = mm(o, xlo[:, k, c0:c0 + P], whi[:, k // 4, w], start=False, stop=k == KT - 1, skip_group_check=True)
                if k % 4 == 3:
                    last.then_inc(E("w_used"), 1)
            pe.wait_ge(E("w_used"), 4)
            pe.wait_ge(E("vecs"), 1)
            pe.wait_ge(E("convw"), 1)
            pe.wait_ge(E("ms"), 1)

            def project(i, at, count):
                for p in range(at, at + count):
                    job, k = p // KT, p % KT
                    n = i * 12 + (HEADS + p // PK)
                    if k == 0 and not isinstance(i, int):
                        pe.wait_ge(E(("z_evac", "v_evac", "qk_evac")[job]), i if job < 2 else i + 1)
                    if k == 0 and isinstance(i, int) and job == 2:
                        pe.wait_ge(E("qk_evac"), 1)
                    if k % PK == 0:
                        pe.wait_ge(E("w_lo"), n + 1)
                    last = k_tile((p // PK) % 4, k % PK, xhi, xlo, k, job % 2, k == 0, k == KT - 1)
                    if k % PK == PK - 1:
                        last.then_inc(E("w_used"), 1)

            def cache_in(i):
                for q in range(4):
                    last = tr(D3[:, 24 * q:24 * q + 24], cc_in[0:24, q, :], ident[0:24, 0:24])
                last.then_inc(E("cc_t"), 1)

            def cache_out(i):
                pe.wait_ge(E("tail"), i + 1)
                pe.wait_ge(E("ident"), 1)
                for q in range(4):
                    last = tr(D3[0:27, P * q:P * q + P], tail[:, q, :], ident[:])
                last.then_inc(E("cc_o"), 1)

            pe.wait_ge(E("gtail"), 1)
            pe.wait_ge(E("consts"), 16)
            one(D1[:, 0:64], shift[:], gtail[:]).then_inc(E("g_pe"), 1)
            project(0, 0, 16)
            pe.wait_ge(E("gg"), 1)
            for q in range(3):
                one(D2[:, 32 * q:32 * q + 32], (tri_p if q < 2 else tri_s)[:], gg[:, q, :])
            for q in range(3):
                one(D2[:, 96 + 32 * q:128 + 32 * q], (ones if q < 2 else blk_s)[:], gg[:, q, :])
            one(D3[:, 0:256], ones[0:64, :], gsb[0:64, :, :].rearrange("p b h -> p (b h)")).then_inc(E("g_pe"), 1)
            project(0, 16, 8)
            pe.wait_ge(E("gct"), 1)
            tr(D1[0:80, 0:P], gct[:], ident[:]).then_inc(E("g_pe"), 1)
            pe.wait_ge(E("t_raw"), 1)
            pe.wait_ge(E("cc_landed"), 48)
            cache_in(0)
            project(0, 24, 16)
            pe.wait_ge(E("cc_evac"), 1)
            cache_out(0)
            project(0, 40, 8)
            pe.wait_ge(E("gcr"), 1)
            pe.wait_ge(E("cc_out"), 1)
            one(D2[:, 0:1], ident[:], ones[:, 0:1]).then_inc(E("pe_round"), 1)

            def delta(n, fill, cached_landed, cached_in, cached_out):
                fill(12)
                rounds(pe, n)
                pe.wait_ge(E("qk_sq"), n)
                for q in range(2):
                    for u in range(3):
                        last = one(D0[:, 3 * q + u:3 * q + u + 1], sq_tok[:, q, P * u:P * u + P], ones[:, 0:1])
                last.then_inc(E("sums_ps"), 1)
                tr(D1[:, 0:P], silu[:, 1, 0:P], ident[:])
                tr(D1[:, P:2 * P], silu[:, 1, P:2 * P], ident[:])
                tr(D1[:, 2 * P:3 * P], samp[:, 1, :], ident[:])
                tr(D1[:, 3 * P:4 * P], samp[:, 2, :], ident[:])
                for u in range(4):
                    last = tr(D2[:, P * u:P * u + P], silu[:, 2 + u // 2, P * (u % 2):P * (u % 2) + P], ident[:])
                last.then_inc(E("kv_ps"), 1)
                fill(3)
                pe.wait_ge(E("k_tok"), n)
                for u in range(3):
                    last = tr(D3[:, P * u:P * u + P], k_tok[:, u, :], ident[:])
                last.then_inc(E("kn_ps"), 1)
                fill(1)
                pe.wait_ge(E("k_t"), n)
                pe.wait_ge(E("sum_sb"), n)
                for u in range(3):
                    last = one(D0[:, P * u:P * u + P], k_t[:, u, :], k_t[:, u, :])
                last.then_inc(E("kk_ps"), 1)
                pe.wait_ge(E("vb"), n)
                for u in range(3):
                    q = silu[:, 0, P * u:P * u + P] if u < 2 else samp[:, 0, :]
                    last = one(D1[:, P * u:P * u + P], q, k_t[:, u, :])
                last.then_inc(E("qk_ps"), 1)
                fill(3)

                def units(dst0, dst1, lhs, rhs, name, samples):
                    for u in range(5 if samples else 4):
                        o = dst0[:, P * u:P * u + P] if u < 4 else dst1[:, 0:P]
                        last = one(o, lhs[:, u, :], rhs[:, u, :])
                    last.then_inc(E(name), 1)

                def turned(dst0, dst1, src, name, samples):
                    for u in range(5 if samples else 4):
                        o = dst0[:, P * u:P * u + P] if u < 4 else dst1[:, 0:P]
                        last = tr(o, src[:, u, :], ident[:])
                    last.then_inc(E(name), 1)

                pe.wait_ge(E("x"), (n - 1) * LEVELS + 1)
                turned(D0, D1, xm, "xt", True)
                fill(1)
                pe.wait_ge(E("a_mat"), n)
                turned(D2, D3, amat, "at_ps", True)
                for k in range(1, LEVELS):
                    s = k < S_LEVELS
                    pe.wait_ge(E("y"), (n - 1) * LEVELS + k)
                    units(D0, D1, lmat, ym, "lp", s)
                    fill(1)
                    pe.wait_ge(E("p"), (n - 1) * (LEVELS - 1) + k)
                    if k == 1:
                        pe.wait_ge(E("a_t"), n)
                    units(D2, D3, p1, xm, f"lx{k}", s)
                    fill(1)
                    if k == 5:
                        cached_landed()
                    pe.wait_ge(E("x"), (n - 1) * LEVELS + (k + 1))
                    turned(D0, D1, xm, "xt", s)
                    if k == 2:
                        pe.wait_ge(E("state_landed"), n * 32)
                        pe.wait_ge(E("x"), (n - 1) * LEVELS + 3)
                        for b in range(NSEQ):
                            for q in range(2):
                                o = D3[:, 0:256].rearrange("p (m v b s) -> p m v b s", m=2, v=2, b=NSEQ)[:, :, q, b, :]
                                last = one(o, s_s[:, b, q, :], kq_in[:, :, SLEN * b:SLEN * b + SLEN])
                        last.then_inc(E("ksqs_ps"), 1)
                    if k == 3:
                        pe.wait_ge(E("ksqs"), n)
                        for q in range(2):
                            last = tr(D3[:, 256 + P * q:384 + P * q], ksqs[:, q, :], ident[:])
                        last.then_inc(E("ksqs_t"), 1)
                    if k == 5:
                        pe.wait_ge(E("ident"), 1)
                        pe.wait_ge(E("o4"), n)
                        cached_in()
                    fill(1)
                pe.wait_ge(E("y"), n * LEVELS)
                pe.wait_ge(E("r4"), n)
                for q, u in enumerate((0, 2, 4)):
                    last = one(D1[:, P * q:P * q + P], ym[:, u, :], vb[:, u, :])
                last.then_inc(E("u0_ps"), 1)
                fill(1)
                pe.wait_ge(E("u0"), n)
                for q, u in enumerate((0, 2, 4)):
                    last = one(D2[:, P * q:P * q + P], a_t[:, u, :], u_m[:, q, :])
                last.then_inc(E("au0_ps"), 1)
                pe.wait_ge(E("ud0"), n)
                one(D0[:, 0:256], k_tok[:, 0, :], ud[:].rearrange("p v c -> p (v c)")).then_inc(E("s0_ps"), 1)
                fill(1)
                pe.wait_ge(E("s0"), n)
                sp2 = s_p[:].rearrange("p v c -> p (v c)")
                one(D1[:, 0:256], k_t[:, 1, :], sp2)
                one(D1[:, 256:512], silu[:, 0, P:2 * P], sp2).then_inc(E("ksqs1"), 1)
                fill(1)
                pe.wait_ge(E("r1"), n)
                pe.wait_ge(E("o_c0"), n)
                for q, u in enumerate((1, 3)):
                    last = one(D2[:, P * q:P * q + P], ym[:, u, :], vb[:, u, :])
                last.then_inc(E("u1_ps"), 1)
                fill(1)
                pe.wait_ge(E("u1"), n)
                for q, u in enumerate((1, 3)):
                    last = one(D0[:, P * q:P * q + P], a_t[:, u, :], u_m[:, q, :])
                last.then_inc(E("au1_ps"), 1)
                pe.wait_ge(E("ud1"), n)
                pe.wait_ge(E("o1"), n)
                one(D1[:, 0:256], k_tok[:, 1, :], ud[:].rearrange("p v c -> p (v c)")).then_inc(E("s1_ps"), 1)
                pe.wait_ge(E("k_m"), n)
                pe.wait_ge(E("ud_s"), n)
                cached_out()
                for q in range(4):
                    if q >= 2:
                        pe.wait_ge(E("ss_sum"), (n - 1) * 4 + (q - 1))
                    bank = (D2, D3)[q % 2]
                    for b in range(2):
                        last = one(bank[:, 256 * b:256 * b + 256], k_m[:, 2 * q + b, :], ud_s[:].rearrange("p v c -> p (v c)"))
                    last.then_inc(E("ss_ps"), 1)
                fill(1)
                pe.wait_ge(E("on"), n)
                pe.wait_ge(E("sp_final"), n)
                turned(D0, D1, o_m, "ot_ps", True)
                fill(None)

            def beside(i):
                at = [0]

                def fill(count):
                    count = 48 - at[0] if count is None else count
                    project(i, at[0], count)
                    at[0] += count
                return fill

            with pe.Fori(1, NH) as i:
                fill = beside(i)

                def cached_landed(i=i):
                    pe.wait_ge(E("cc_landed"), i * 48 + 48)

                def cached_in(i=i):
                    cache_in(i)

                def cached_out(i=i):
                    pe.wait_ge(E("cc_evac"), i + 1)
                    cache_out(i)
                    pe.wait_ge(E("cc_out"), i + 1)
                delta(i, fill, cached_landed, cached_in, cached_out)
                one(D2[:, 0:1], ident[:], ones[:, 0:1]).then_inc(E("pe_round"), 1)
            delta(NH, lambda count: None, lambda: None, lambda: None, lambda: None)
            one(D2[:, 0:1], ident[:], ones[:, 0:1]).then_inc(E("pe_round"), 1)

    def norm_act(act, r, tiles):
        act.wait_ge(E("ms"), r + 1)
        nc.scalar.activation(rb2[:], rb2[:], ACT.Sqrt).then_inc(E("rms"), 1)
        for k in range(tiles):
            act.wait_ge(E("xnorm"), KT * r + k + 1)
            nc.scalar.activation(xhi[:, k, :], xn[:, k % 4, :], ACT.Copy).then_inc(E("x_hi"), 1)

    def norm_scale(dve, r):
        dve.wait_ge(E("ssum"), 10 * r)
        nc.vector.tensor_scalar(rb2[:], D0[:, 0:T], 1.0 / DM, EPS, ALU.mult, ALU.add).then_inc(E("ms"), 1)
        dve.wait_ge(E("rms"), r + 1)
        nc.vector.reciprocal(rb2[:], rb2[:]).then_inc(E("rinv"), 1)
        dve.wait_ge(E("rinv"), r + 1)

    def norm_tile(dve, r, k):
        nc.vector.scalar_tensor_tensor(xn[:, k % 4, :], ht[:, k, :], vecs[:, KT * r + k:KT * r + k + 1], rb2[:],
                                       ALU.mult, ALU.mult).then_inc(E("xnorm"), 1)

    def odd_out(v, dve, k):
        dve.wait_ge(E("tiles_t"), KT + k + 1)
        v.tensor_copy(ytok[:, 0:2, P * k:P * k + P], blocks(ps[:, k % 4, 0:256], 2))
        v.tensor_copy(ytok[0:64, 2, P * k:P * k + P], ps[0:64, k % 4, 256:384]).then_inc(E("odd_tiles"), 1)

    def output_projection(first, w3, job0, r):
        last_phase = r == 2
        split_base = 8 * (r - 1)
        with nc.Block() as block:
            @block.sync
            def _(sp):
                if r == 1:
                    sp.wait_ge(E("ht_saved"), 16)
                    sp.dma_start(ht[:].rearrange("p k t -> p (k t)"), ht_dram).then_inc(E("ht_in"), 16)
                for half in range(2):
                    with sp.Fori(1 - half, 8) as j:
                        for pc in range(4):
                            load(sp, j * 4 + (first + 32 * half + pc), pc, one_block(pc, w3, KT * half + PK * pc, j * 256))
                if not last_phase:
                    sp.wait_ge(E("cc_dma"), 96 * NH)
                    sp.wait_ge(E("delta_out"), 48 * NH + 16)
                    for pc in range(4):
                        load(sp, first + 64 + pc, pc, one_block(pc, pw_in, PK * pc, 0))
                if last_phase:
                    for ch in range(4):
                        c = slice(512 * ch, 512 * ch + 512)
                        sp.wait_ge(E("even_tiles"), KT // 2 + 2 * ch + 2)
                        sp.wait_ge(E("odd_tiles"), KT // 2 + 2 * ch + 2)
                        for g_ in range(2):
                            sp.dma_start(y_prompt[0, P * g_:P * g_ + P, c], ytok[:, g_, c]).then_inc(E("rows_out"), 16)
                        sp.dma_start(y_sample.rearrange("b s c -> (b s) c")[:, c], ytok[0:64, 2, c]).then_inc(E("rows_out"), 16)
                    sp.wait_ge(E("rows_out"), 12 * 16)
                    sp.wait_ge(E("cc_dma"), 96 * NH)
                    sp.wait_ge(E("delta_out"), 48 * NH + 16)
                    sp.wait_ge(E("cp_dma"), 32 * NH + 16)

            @block.gpsimd
            def _(pool):
                nc.gpsimd.memset(sqp[:, 1, :, :], 0.0).then_inc(E("sqp"), 1)

            @block.scalar
            def _(act):
                sc = nc.scalar
                for half in range(2):
                    for ch in range(4):
                        if ch == 0:
                            act.wait_ge(E("w_used"), first + 32 * half)
                        k0 = KT * half + 4 * ch
                        sc.activation(xhi[:, 4 * ch:4 * ch + 4, :], branch[:, k0:k0 + 4, :], ACT.Copy).then_inc(E("b_hi"), 1)
                    clipped = last_phase and half == 1

                    def splits(j, count, half=half):
                        for pc in range(count):
                            split_hi(act, j * 4 + (first + 32 * half + LEAD + pc), (LEAD + pc) % 4)

                    def square(i, jb):
                        act.wait_ge(E(f"free{jb}"), i + (job0 + 8) // 2 + 2)
                        act.wait_ge(E("ssum"), i * 2 + (10 * (r - 1) + jb + 1))
                        sc.activation(sqp[:, jb, :, :], ht[:, bass.ds(i * 4 + 2 * jb, 2), :], ACT.Square).then_inc(E("sqp"), 1)

                    with act.Fori(0, 3 if clipped else 4) as i:
                        for jb in range(2):
                            splits(i * 2 + jb, 4)
                            if half == 1:
                                square(i, jb)
                    if clipped:
                        splits(6, 4)
                        square(3, 0)
                        splits(7, 2)
                        square(3, 1)
                norm_act(act, r, 0 if last_phase else KT)
                if last_phase:
                    for k in range(0, KT, 2):
                        act.wait_ge(E("tiles_t"), KT + k + 1)
                        sc.activation(ytok[:, 0:2, P * k:P * k + P], blocks(ps[:, k % 4, 0:256], 2), ACT.Copy)
                        sc.activation(ytok[0:64, 2, P * k:P * k + P], ps[0:64, k % 4, 256:384], ACT.Copy
                                      ).then_inc(E("even_tiles"), 1)

            @block.vector
            def _(dve):
                v = nc.vector
                if r == 1:
                    for pair in range(2):
                        v.tensor_copy(small[:, pair:pair + 1], ones[:, 0:1]).then_inc(E(f"free{pair}"), 1)
                    dve.wait_ge(E("ht_in"), 16)
                for half in range(2):
                    for ch in range(4):
                        k0 = KT * half + 4 * ch
                        dve.wait_ge(E("b_hi"), split_base + 4 * half + ch + 1)
                        v.tensor_tensor(xlo[:, 4 * ch:4 * ch + 4, :], branch[:, k0:k0 + 4, :],
                                        xhi[:, 4 * ch:4 * ch + 4, :].bitcast(F32), ALU.subtract).then_inc(E("b_lo"), 1)
                    clipped = last_phase and half == 1

                    def job(i, jb, count, half=half):
                        for pc in range(count):
                            split_lo(dve, i * 8 + (first + 32 * half + 4 * jb + LEAD + pc), (LEAD + pc) % 4)
                        if half == 1:
                            dve.wait_ge(E(f"free{jb}"), i + (job0 // 2 + 2))
                        dve.wait_ge(E("w_used"), i * 8 + (first + 32 * half + 4 * jb + 4))
                        tiles = ht[:, bass.ds(i * 4 + 2 * jb, 2), :]
                        v.tensor_tensor(tiles, ps[:, 2 * jb:2 * jb + 2, 0:T], tiles, ALU.add).then_inc(E(f"free{jb}"), 1)

                    with dve.Fori(0, 3 if clipped else 4) as i:
                        for jb in range(2):
                            job(i, jb, 4)
                    if clipped:
                        job(3, 0, 4)
                        job(3, 1, 2)
                norm_scale(dve, r)
                for k in range(KT):
                    if k >= 4:
                        if last_phase:
                            dve.wait_ge(E("tiles_t"), KT + k - 3)
                        else:
                            dve.wait_ge(E("x_lo"), KT * r + k - 3)
                    norm_tile(dve, r, k)
                    if not last_phase and k >= 1:
                        dve.wait_ge(E("x_hi"), KT * r + k)
                        v.tensor_tensor(xlo[:, k - 1, :], xn[:, (k - 1) % 4, :], xhi[:, k - 1, :].bitcast(F32), ALU.subtract
                                        ).then_inc(E("x_lo"), 1)
                    if last_phase and k % 2 == 0 and k >= 2:
                        odd_out(v, dve, k - 1)
                if last_phase:
                    odd_out(v, dve, KT - 1)
                else:
                    dve.wait_ge(E("x_hi"), KT * r + KT)
                    v.tensor_tensor(xlo[:, KT - 1, :], xn[:, (KT - 1) % 4, :], xhi[:, KT - 1, :].bitcast(F32), ALU.subtract
                                    ).then_inc(E("x_lo"), 1)

            @block.tensor
            def _(pe):
                mm = nc.tensor.matmul

                def add_squares(jb, i, stop=False):
                    pe.wait_ge(E("sqp"), i * 2 + (9 * (r - 1) + 1 + jb))
                    mm(D0[:, 0:T], ones[:], sqp[:, 1 - jb, 0, :], start=False, stop=False)
                    mm(D0[:, 0:T], ones[:], sqp[:, 1 - jb, 1, :], start=False, stop=stop).then_inc(E("ssum"), 1)

                pe.wait_ge(E("sqp"), 9 * (r - 1) + 1)
                mm(D0[:, 0:T], ones[:], sqp[:, 1, 0, :], start=True, stop=False).then_inc(E("ssum"), 1)
                for half in range(2):
                    with pe.Fori(0, 4) as i:
                        for jb in range(2):
                            pe.wait_ge(E(f"free{jb}"), i + (job0 // 2 + 4 * half + 1))
                            for pc in range(4):
                                pe.wait_ge(E("w_lo"), i * 8 + (first + 32 * half + 4 * jb + pc + 1))
                                pe.wait_ge(E("b_lo"), split_base + 4 * half + pc + 1)
                                for k in range(4):
                                    last = k_tile(pc, k, xhi, xlo, 4 * pc + k, jb, pc + k == 0, pc + k == 6)
                                last.then_inc(E("w_used"), 1)
                            if half == 1:
                                add_squares(jb, i)
                add_squares(0, 4, True)
                if last_phase:
                    for k in range(KT):
                        pe.wait_ge(E("xnorm"), KT * r + k + 1)
                        if k >= 4:
                            pe.wait_ge(E("odd_tiles" if k % 2 else "even_tiles"), KT // 2 + (k - 4) // 2 + 1)
                        b = ps[:, k % 4, :]
                        x = xn[:, k % 4, :]
                        nc.tensor.transpose(b[:, 0:P], x[:, 0:P], ident[:])
                        nc.tensor.transpose(b[:, P:2 * P], x[:, P:2 * P], ident[:])
                        nc.tensor.transpose(b[0:64, 2 * P:3 * P], x[:, 2 * P:T], ident[:]).then_inc(E("tiles_t"), 1)

    output_projection(OUT_A, w_out, 0, 1)

    with nc.Block() as block:
        def z_cols(gi, t):
            return t * 256 + (1024 * gi + DI)

        @block.sync
        def _(sp):
            sp.dma_start(new_cp_s[0, :, 0:PB - SLEN, :], cache_pool[0, :, SLEN:PB, :]).then_inc(E("cp_dma"), 16)
            cp = cache_pool[0].rearrange("b r c -> (b r) c")
            for gi in range(NG):
                base = POOL + 40 * gi
                wg = pool_w_group[0, gi].rearrange("(k p) c -> p k c", p=P)

                def cached_and_z(t):
                    sp.wait_ge(E("cp_t"), t + (4 * gi + 1))
                    sp.dma_start(cp_in[0:NSEQ * PB, :], cp[:, bass.ds(t * 256 + 1024 * gi, 256)]).then_inc(E("cp_landed"), 16)
                    for pc in range(4):
                        load(sp, t * 8 + (base + 4 + pc), pc, one_block(pc, pw_in, PK * pc, z_cols(gi, t)))

                with sp.Fori(0, 3) as t:
                    cached_and_z(t)
                    for pc in range(4):
                        load(sp, t * 8 + (base + 8 + pc), pc, one_block(pc, pw_in, PK * pc, t * 256 + (1024 * gi + 256)))
                cached_and_z(3)
                for q in range(8):
                    load(sp, base + 32 + q, q % 4, one_block(q % 4, wg, PK * (q % 2), 256 * (q // 2)))
                for pc in range(4):
                    c1 = 1024 * (gi + 1) if gi + 1 < NG else 0
                    load(sp, base + 40 + pc, pc, one_block(pc, pw_in if gi + 1 < NG else pw_out, PK * pc, c1))

        @block.gpsimd
        def _(pool):
            gp = nc.gpsimd
            gp.memset(ubuf[:, :, 0:PB], 0.0).then_inc(E("pool_zero"), 1)
            for gi, win in enumerate(WINDOWS):
                for t in range(PB):
                    gp.memset(rcount[:, gi, t:t + 1], 1.0 / min(t + 1, win))
            gp.memset(rcount[:, :, PB:PB + 1], 1.0).then_inc(E("rcount"), 1)

        @block.scalar
        def _(act):
            sc = nc.scalar
            for c, name in enumerate(("ptail", "cp_out")):
                sc.activation(small[:, 8 + c:9 + c], ones[:, 0:1], ACT.Copy).then_inc(E(name), 1)
            for gi in range(NG):
                base, g4 = POOL + 40 * gi, 4 * gi

                def split(t, q):
                    split_hi(act, t * 8 + (base + LEAD + q), (LEAD + q) % 4)

                with act.Fori(0, 4) as t:
                    for q in range(3):
                        split(t, q)
                    act.wait_ge(E("pooled"), t + (g4 + 1))
                    act.wait_ge(E("cp_t"), t + (g4 + 2))
                    sc.activation(pool_strips(ubuf, 0, PB), blocks(D1[:, 0:256], 2)[:, :, 0:NSEQ * PB].rearrange(
                        "p n (b r) -> p n b r", b=NSEQ), ACT.Copy)
                    split(t, 3)
                    act.wait_ge(E("w_used"), t * 8 + (base + 4))
                    sc.activation(ubuf[:, :, PB:PS_AT], ps[:, 0:2, 0:NPT], ACT.Copy)
                    sc.activation(pool_strips(ubuf, PB, SLEN), toks(ps[:, 0:2, NPT:T]), ACT.Copy).then_inc(E("free0"), 1)
                    act.wait_ge(E("free0"), t + (J_POOL // 2 + 6 * gi + 2))
                    act.wait_ge(E("cp_o"), t + (g4 + 1))
                    sc.activation(toks(ptail[:, :, 0:64]), pool_strips(ubuf, PB, SLEN), ACT.Copy)
                    sc.activation(ptail[:, :, 64:79], ubuf[:, :, NPT:NPT + PB], ACT.Copy).then_inc(E("ptail"), 1)
                    split(t, 4)
                    split(t, 5)
                    act.wait_ge(E("pooled"), t + (g4 + 2))
                    act.wait_ge(E("w_used"), base)
                    sc.activation(phi[:, bass.ds(t * 2, 2), :], pooled[:], ACT.Copy).then_inc(E("p_hi"), 1)
                    act.wait_ge(E("cp_o"), t + (g4 + 2))
                    act.wait_ge(E("cp_dma"), t * 32 + (32 * g4 + 16))
                    sc.activation(cp_out[0:79, :], D2[0:79, 0:256], ACT.Copy).then_inc(E("cp_out"), 1)
                    act.wait_ge(E("cp_out"), t + (g4 + 2))
                    c = bass.ds(t * 256 + 1024 * gi, 256)
                    act.dma_start(new_cp_s[0, :, PB - SLEN:PB, c], cp_out[0:64, :]).then_inc(E("cp_dma"), 16)
                    act.dma_start(new_cp_p[0, 0, :, c], cp_out[64:79, :]).then_inc(E("cp_dma"), 16)
                    split(t, 6)
                    split(t, 7)
                    act.wait_ge(E("w_used"), t * 8 + (base + 8))
                    act.wait_ge(E("s2z"), t + (g4 + 1))
                    sc.activation(ztanh[:], ps[:, 2:4, 0:T], ACT.Tanh, scale=0.5).then_inc(E("ztanh"), 1)
                for q in range(8):
                    split(4, q)

        @block.vector
        def _(dve):
            v = nc.vector
            for c, name in enumerate(("pooled", "s2z", "p_lo")):
                v.tensor_copy(small[:, 1 + c:2 + c], ones[:, 0:1]).then_inc(E(name), 1)
            for gi, win in enumerate(WINDOWS):
                base, g4 = POOL + 40 * gi, 4 * gi
                adds = gi + 1

                def split(t, q):
                    split_lo(dve, t * 8 + (base + LEAD + q), (LEAD + q) % 4)

                def sums_before(k):
                    return k * (k + 1) // 2 * 4

                with dve.Fori(0, 4) as t:
                    for q in range(4):
                        split(t, q)
                    dve.wait_ge(E("free0"), t + (J_POOL // 2 + 6 * gi + 2))
                    dve.wait_ge(E("pool_zero"), 1)
                    src, at = ubuf, t * adds + sums_before(gi)
                    for a in range(adds):
                        n = PW - (2 << a) + 1
                        dst = (ws_a, ws_b)[a % 2]
                        if a:
                            dve.wait_ge(E("wsum"), t * adds + (sums_before(gi) + a))
                        v.tensor_tensor(dst[:, :, 0:n], src[:, :, 0:n], src[:, :, (1 << a):(1 << a) + n], ALU.add
                                        ).then_inc(E("wsum"), 1)
                        src = dst
                        if a == 0:
                            split(t, 4)
                    dve.wait_ge(E("p_lo"), t + (g4 + 1))
                    dve.wait_ge(E("rcount"), 1)
                    dve.wait_ge(E("wsum"), t * adds + (sums_before(gi) + adds))
                    o = PB + 1 - win
                    v.scalar_tensor_tensor(pooled[:, :, PB:NPT], src[:, :, o + PB:o + NPT], 1.0 / win, ubuf[:, :, 2 * PB:PS_AT],
                                           ALU.mult, ALU.subtract)
                    for h in range(2):
                        v.scalar_tensor_tensor(toks(pooled[:, h:h + 1, NPT:T])[:, 0], pool_strips(src, o, SLEN)[:, h], 1.0 / win,
                                               pool_strips(ubuf, PB, SLEN)[:, h], ALU.mult, ALU.subtract)
                    v.tensor_tensor(pooled[:, :, 0:PB], src[:, :, o:o + PB], rcount[:, gi:gi + 1, 0:PB].to_broadcast([P, 2, PB]),
                                    ALU.mult).then_inc(E("pfirst"), 1)
                    dve.wait_ge(E("pfirst"), t + (g4 + 1))
                    v.tensor_tensor(pooled[:, :, 0:PB], pooled[:, :, 0:PB], ubuf[:, :, PB:2 * PB], ALU.subtract
                                    ).then_inc(E("pooled"), 1)
                    split(t, 5)
                    dve.wait_ge(E("p_hi"), t + (g4 + 1))
                    v.tensor_tensor(plo[:, bass.ds(t * 2, 2), :], pooled[:], phi[:, bass.ds(t * 2, 2), :].bitcast(F32),
                                    ALU.subtract).then_inc(E("p_lo"), 1)
                    split(t, 6)
                    split(t, 7)
                    dve.wait_ge(E("ztanh"), t + (g4 + 1))
                    v.scalar_tensor_tensor(s2z[:, bass.ds(t * 2, 2), :], ztanh[:], 1.0, ps[:, 2:4, 0:T], ALU.add, ALU.mult
                                           ).then_inc(E("s2z"), 1)
                    dve.wait_ge(E("s2z"), t + (g4 + 2))
                    v.tensor_copy(small[:, 0:1], ones[:, 0:1]).then_inc(E("free1"), 1)
                for jb in range(4):
                    split(4, 2 * jb)
                    split(4, 2 * jb + 1)
                    dve.wait_ge(E("w_used"), base + 32 + 2 * jb + 2)
                    for h in range(2):
                        k = 8 * gi + 2 * jb + h
                        last = v.scalar_tensor_tensor(branch[:, k, :], ps[:, 2 * (jb % 2) + h, 0:T],
                                                      vecs[:, V_SCALE + k:V_SCALE + k + 1], s2z[:, 2 * jb + h, :],
                                                      ALU.mult, ALU.mult)
                    last.then_inc(E(f"free{jb % 2}"), 1)

        @block.tensor
        def _(pe):
            for c, name in enumerate(("cp_t", "cp_o")):
                nc.tensor.matmul(D3[:, c:c + 1], ident[:], ones[:, 0:1], start=True, stop=True).then_inc(E(name), 1)
            for gi in range(NG):
                base, g4, job = POOL + 40 * gi, 4 * gi, J_POOL // 2 + 6 * gi

                def pieces(t, q, count, pair):
                    for pc in range(q, q + count):
                        pe.wait_ge(E("w_lo"), t * 8 + (base + pc + 1))
                        if gi == 0:
                            pe.wait_ge(E("x_lo"), KT + 4 * (pc % 4) + 4)
                        for k in range(4):
                            kk = 4 * (pc % 4) + k
                            last = k_tile(pc % 4, k, xhi, xlo, kk, pair, kk == 0, kk == KT - 1)
                        last.then_inc(E("w_used"), 1)

                with pe.Fori(0, 4) as t:
                    pe.wait_ge(E("free0"), t + (job + 1))
                    pieces(t, 0, 2, 0)
                    pe.wait_ge(E("cp_landed"), t * 16 + (64 * gi + 16))
                    pe.wait_ge(E("ptail"), t + (g4 + 1))
                    for h in range(2):
                        last = nc.tensor.transpose(D1[:, P * h:P * h + NSEQ * PB], cp_in[0:NSEQ * PB, P * h:P * h + P],
                                                   ident[0:NSEQ * PB, 0:NSEQ * PB])
                    last.then_inc(E("cp_t"), 1)
                    pieces(t, 2, 2, 0)
                    pe.wait_ge(E("free1"), t + (job + 1))
                    pieces(t, 4, 2, 1)
                    pe.wait_ge(E("ptail"), t + (g4 + 2))
                    pe.wait_ge(E("cp_out"), t + (g4 + 1))
                    for h in range(2):
                        last = nc.tensor.transpose(D2[0:79, P * h:P * h + P], ptail[:, h, :], ident[:])
                    last.then_inc(E("cp_o"), 1)
                    pieces(t, 6, 2, 1)
                pe.wait_ge(E("p_lo"), g4 + 5)
                for jb in range(4):
                    pe.wait_ge(E(f"free{jb % 2}"), job + 4 + jb // 2 + 1)
                    for pc in range(2):
                        pe.wait_ge(E("w_lo"), base + 32 + 2 * jb + pc + 1)
                        for k in range(4):
                            kk = 4 * pc + k
                            last = k_tile((2 * jb + pc) % 4, k, phi, plo, kk, jb % 2, kk == 0, kk == 7)
                        last.then_inc(E("w_used"), 1)

    output_projection(OUT_B, pw_out, J_OUT_B, 2)


_INS = ("x_prompt", "x_sample", "state_delta", "cache_conv", "cache_pool", "norm_w", "final_norm_w", "delta_w_in",
        "delta_conv_w", "delta_a_log", "delta_dt_bias", "delta_o_norm_w", "delta_w_out", "pool_w_in", "pool_w_group",
        "pool_scale", "pool_w_out")
_OUTS = ((1, NPT, DM), (NSEQ, SLEN, DM), (1, 1, 2 * NH, P, P), (1, 1, TAPS - 1, QKV), (1, 1, PB, DI),
         (1, NSEQ, 2 * NH, P, P), (1, NSEQ, TAPS - 1, QKV), (1, NSEQ, PB, DI))


def kernel(**inputs):
    import numpy as _np
    import concourse.bacc as _bacc
    from concourse import mybir as _mybir
    from concourse.bass_utils import run_bass_kernel_spmd as _run

    nc = _bacc.Bacc("TRN2", target_bir_lowering=False, num_devices=1)
    arrays, args = {}, []
    for name in _INS:
        a = _np.ascontiguousarray(inputs[name])
        arrays[f"in_{name}_dram"] = a
        args.append(nc.dram_tensor(f"in_{name}_dram", a.shape, _mybir.dt.from_np(a.dtype), kind="ExternalInput").ap())
    for i, shape in enumerate(_OUTS):
        args.append(nc.dram_tensor(f"out_{i}_dram", shape, _mybir.dt.float32, kind="ExternalOutput").ap())
    build(nc, *args)
    r = _run(nc, [arrays], core_ids=[0])
    return tuple(r.results[0][f"out_{i}_dram"] for i in range(len(_OUTS)))
```

```python
import concourse.bass as bass
from concourse import mybir

P = 128
NPT, NSEQ, SLEN = 256, 8, 8
T = NPT + NSEQ * SLEN
DM, DI = 2048, 4096
KT = DM // P
NH = DM // P
QKV = 2 * DM + DI
TAPS = 4
SW = SLEN + TAPS - 1
S_AT = NPT + TAPS - 1
CW = S_AT + NSEQ * SW
CV = CW - (TAPS - 1)
WINDOWS = (2, 4, 8, 16)
NG = len(WINDOWS)
PB = max(WINDOWS) - 1
PSW = SLEN + PB
PS_AT = PB + NPT
PW = PS_AT + NSEQ * PSW
EPS = 1e-6
NEG = -1e30
LEVELS = 7
S_LEVELS = 3
PK = 4
LEAD = 2

F32, F32R, U8 = mybir.dt.float32, mybir.dt.float32r, mybir.dt.uint8
ALU = mybir.AluOpType
ACT = mybir.ActivationFunctionType

HEADS = 4
OUT_A = HEADS + 12 * NH
POOL = OUT_A + 64
OUT_B = POOL + 40 * NG
J_POOL = 16
J_OUT_B = J_POOL + 12 * NG

V_SCALE, V_O = 3 * KT, 5 * KT
GC, NBETA, HBETA, NBE, EGC, DEC = (5 * k for k in range(6))
EGL = 30


def build(nc, x_prompt, x_sample, state_delta, cache_conv, cache_pool, norm_w, final_norm_w, delta_w_in,
          delta_conv_w, delta_a_log, delta_dt_bias, delta_o_norm_w, delta_w_out, pool_w_in, pool_w_group,
          pool_scale, pool_w_out, y_prompt, y_sample, new_sd_p, new_cc_p, new_cp_p, new_sd_s, new_cc_s, new_cp_s):
    def place(at, name, shape, dt=F32):
        size = 1 if dt == U8 else 4
        for n in shape:
            size *= n
        t = nc.alloc_sbuf_tensor_at(name, [P] + list(shape), dt, offset=at[0])
        at[0] += (size + 31) // 32 * 32
        return t

    m = [(nc.sbuf_base + 31) // 32 * 32]
    xhi = place(m, "xhi", [KT, T], F32R)
    xlo = place(m, "xlo", [KT, T], F32R)
    wraw = place(m, "wraw", [4, PK * 256])
    whi = place(m, "whi", [4, PK * 256], F32R)
    wlo = place(m, "wlo", [4, PK * 256], F32R)
    branch = place(m, "branch", [2 * KT, T])
    ident = place(m, "ident", [P])
    ones = place(m, "ones", [P])
    mask_p = place(m, "mask_p", [P])
    mask_s = place(m, "mask_s", [P])
    level = place(m, "level", [LEVELS, P], U8)
    seqmask = place(m, "seqmask", [NSEQ])
    minushalf = place(m, "minushalf", [8])
    vecs = place(m, "vecs", [96])
    convw = place(m, "convw", [NH, 4, TAPS])
    table = place(m, "table", [NH, 50])
    small = place(m, "small", [64])
    shared = m[0]

    a = [shared]
    convin = place(a, "convin", [4, CW])
    zraw = place(a, "zraw", [2, T])
    cc_in = place(a, "cc_in", [4, P])
    cc_out = place(a, "cc_out", [4, P])
    tail = place(a, "tail", [4, 27])
    silu = place(a, "silu", [4, CV])
    convout = place(a, "convout", [4, CV])
    gate = place(a, "gate", [2, T])
    samp = place(a, "samp", [3, P])
    k_tok = place(a, "k_tok", [3, P])
    k_t = place(a, "k_t", [3, P])
    qk_r = place(a, "qk_r", [3, P])
    vb = place(a, "vb", [5, P])
    dec = place(a, "dec", [5, P])
    lmat = place(a, "lmat", [5, P])
    xm = place(a, "xm", [5, P])
    ym = place(a, "ym", [5, P])
    p1 = place(a, "p1", [5, P])
    amat = place(a, "amat", [5, P])
    a_t = place(a, "a_t", [5, P])
    k_m = place(a, "k_m", [NSEQ, P])
    s_s = place(a, "s_s", [NSEQ, 2, P])
    s_p = place(a, "s_p", [2, P])
    ud_s = place(a, "ud_s", [2, P])
    ud = place(a, "ud", [2, P])
    u_m = place(a, "u_m", [3, P])
    kq_in = place(a, "kq_in", [2, NSEQ * SLEN])
    ksqs = place(a, "ksqs", [2, P])
    o_m = amat
    cur = place(a, "cur", [50])
    cwcur = place(a, "cwcur", [4, TAPS])
    gc_next = place(a, "gc_next", [5])
    g = [shared]
    ht = place(g, "ht", [KT, T])
    xtok = place(g, "xtok", [3, DM])
    sq = place(g, "sq", [4, T])
    rb = place(g, "rb", [T])
    vrow = place(g, "vrow", [P])
    crow = place(g, "crow", [2, P])
    lv = place(g, "lv", [LEVELS, P])
    tri_p = place(g, "tri_p", [P])
    tri_s = place(g, "tri_s", [P])
    blk_s = place(g, "blk_s", [P])
    shift = place(g, "shift", [P])
    graw = place(g, "graw", [3, 64])
    gtail = place(g, "gtail", [64])
    gfeat = place(g, "gfeat", [T])
    gvec = place(g, "gvec", [2, 32])
    gt = place(g, "gt", [3, 32])
    gy = place(g, "gy", [3, 32])
    ge = place(g, "ge", [3, 32])
    gg = place(g, "gg", [3, 32])
    gcs = place(g, "gcs", [3, 32])
    gsb = place(g, "gsb", [NSEQ, 32])
    gct = place(g, "gct", [80])
    gcr = place(g, "gcr", [P])
    c = [shared + KT * T * 4]
    sqp = place(c, "sqp", [2, 2, T])
    rb2 = place(c, "rb2", [T])
    xn = place(c, "xn", [4, T])
    ytok = place(c, "ytok", [3, DM])
    w = [shared + KT * T * 4]
    phi = place(w, "phi", [8, T], F32R)
    plo = place(w, "plo", [8, T], F32R)
    s2z = place(w, "s2z", [8, T])
    ubuf = place(w, "ubuf", [2, PW])
    ws_a = place(w, "ws_a", [2, PW])
    ws_b = place(w, "ws_b", [2, PW])
    pooled = place(w, "pooled", [2, T])
    ztanh = place(w, "ztanh", [2, T])
    cp_in = place(w, "cp_in", [256])
    cp_out = place(w, "cp_out", [256])
    ptail = place(w, "ptail", [2, 79])
    rcount = place(w, "rcount", [NG, PB + 1])
    assert max(a[0], g[0], c[0], w[0]) <= nc.sbuf_usable_end

    ps = nc.alloc_psum_tensor("ps", [P, 8, 512], F32)
    D0, D1, D2, D3 = (ps[:, n, :] for n in (4, 5, 6, 7))
    ht_dram = nc.dram_tensor("ht_save", (P, KT * T), F32, kind="Internal").ap()
    gc_dram = nc.dram_tensor("gc_rows", (NH * 5, P), F32, kind="Internal").ap()

    sems = {}

    def E(name):
        if name not in sems:
            sems[name] = nc.alloc_semaphore(name)
        return sems[name]

    w_in = delta_w_in[0].rearrange("(k p) c -> p k c", p=P)
    w_out = delta_w_out[0].rearrange("(k p) c -> p k c", p=P)
    pw_in = pool_w_in[0].rearrange("(k p) c -> p k c", p=P)
    pw_out = pool_w_out[0].rearrange("(k p) c -> p k c", p=P)
    ENG = ("pe", "act", "dve", "pool")

    def rounds(eng, n):
        for e in ENG:
            eng.wait_ge(E(f"{e}_round"), n)

    def blocks(v, n):
        return v.rearrange("p (u c) -> p u c", u=n)

    def wide(v, n):
        return v.rearrange("p (u o) -> p u o", o=1).to_broadcast([P, n, P])

    def conv_strips(t, n0, n1, skip, take):
        v = t[:, n0:n1, S_AT:].rearrange("p n (b s) -> p n b s", s=SW)
        return v[:, :, :, skip:skip + take]

    def sample_cols(n0, n1):
        return silu[:, n0:n1, NPT:CV].rearrange("p n (b s) -> p n b s", s=SW)[:, :, :, TAPS - 1:]

    def toks(v):
        return v.rearrange("p n (b s) -> p n b s", s=SLEN)

    def pool_strips(t, skip, take):
        return t[:, :, PS_AT:].rearrange("p n (b s) -> p n b s", s=PSW)[:, :, :, skip:skip + take]

    def load(sp, n, slot, halves):
        if not (isinstance(n, int) and n < 4):
            sp.wait_ge(E("w_hi"), n - 3)
            sp.wait_ge(E("w_lo"), n - 3)
        for dst, src in halves:
            sp.dma_start(dst, src).then_inc(E(f"w_landed{slot}"), 16)

    def one_block(slot, w3, k0, c1):
        dst = wraw[:, slot, :].rearrange("p (k c) -> p k c", k=PK)
        return ((dst[:, 0:2, :], w3[:, k0:k0 + 2, bass.ds(c1, 256)]),
                (dst[:, 2:4, :], w3[:, k0 + 2:k0 + 4, bass.ds(c1, 256)]))

    def split_hi(act, n, slot, width=1024):
        act.wait_ge(E(f"w_landed{slot}"), (n - slot) * 8 + 32)
        if not (isinstance(n, int) and n < 4):
            act.wait_ge(E("w_used"), n - 3)
        nc.scalar.activation(whi[:, slot, 0:width], wraw[:, slot, 0:width], ACT.Copy).then_inc(E("w_hi"), 1)

    def split_lo(dve, n, slot, width=1024):
        dve.wait_ge(E("w_hi"), n + 1)
        nc.vector.tensor_tensor(wlo[:, slot, 0:width], wraw[:, slot, 0:width], whi[:, slot, 0:width].bitcast(F32),
                                ALU.subtract).then_inc(E("w_lo"), 1)

    def k_tile(slot, k_w, hi, lo, k_x, pair, first, last):
        mm = nc.tensor.matmul
        for h in range(2):
            w = slice(256 * k_w + P * h, 256 * k_w + P * h + P)
            o = ps[:, 2 * pair + h, 0:T]
            mm(o, whi[:, slot, w], hi[:, k_x, :], start=first, stop=False)
            mm(o, whi[:, slot, w], lo[:, k_x, :], start=False, stop=False)
            done = mm(o, wlo[:, slot, w], hi[:, k_x, :], start=False, stop=last)
        return done

    sq_tok = convout[:].rearrange("p n c -> p (n c)")[:, 0:768].rearrange("p (m c) -> p m c", m=2)

    with nc.Block() as block:
        @block.sync
        def _(sp):
            def two_blocks(slot, k0, c1, c2):
                dst = wraw[:, slot, :].rearrange("p (k c) -> p k c", k=PK)
                return ((dst[:, :, 0:P], w_in[:, k0:k0 + PK, bass.ds(c1, P)]),
                        (dst[:, :, P:2 * P], w_in[:, k0:k0 + PK, bass.ds(c2, P)]))

            sp.dma_start(xtok[:, 0, :], x_prompt[0, 0:P, :]).then_inc(E("x_in"), 16)
            sp.dma_start(xtok[:, 1, :], x_prompt[0, P:2 * P, :]).then_inc(E("x_in"), 16)
            sp.dma_start(xtok[0:64, 2, :], x_sample.rearrange("b s c -> (b s) c")).then_inc(E("x_in"), 16)
            for src, r, n in ((norm_w.rearrange("n (k c) -> (n k) c", c=P), 0, 32),
                              (final_norm_w.rearrange("(k c) -> k c", c=P), 32, 16),
                              (pool_scale[0].rearrange("(k c) -> k c", c=P), 48, 32), (delta_o_norm_w, 80, 1)):
                sp.dma_start(vrow[r:r + n, :], src).then_inc(E("rows_in"), 16)
            for h in range(2):
                sp.dma_start(crow[:, h, :], delta_conv_w[0, 2 * h:2 * h + 2, :].rearrange(
                    "j (n c) -> (j n) c", c=P)).then_inc(E("rows_in"), 16)
            sp.dma_start(gvec[:, 0, :], delta_a_log[0].partition_broadcast(P)).then_inc(E("gvec_in"), 16)
            sp.dma_start(gvec[:, 1, :], delta_dt_bias[0].partition_broadcast(P)).then_inc(E("gvec_in"), 16)
            for j in range(4):
                dst = wraw[:, j, 0:512].rearrange("p (k c) -> p k c", k=PK)
                src = w_in[:, PK * j:PK * j + PK, QKV + DI - 64:QKV + DI + 64]
                load(sp, j, j, ((dst[:, 0:2, :], src[:, 0:2, :]), (dst[:, 2:4, :], src[:, 2:4, :])))

            def cache_rows(i):
                cc = cache_conv[0].rearrange("b r c -> (b r) c")
                for n0, n1, c0 in ((0, 1, i * P), (1, 2, i * P + DM), (2, 4, i * 256 + 2 * DM)):
                    sp.dma_start(cc_in[0:24, n0:n1, :].rearrange("p n c -> p (n c)"), cc[:, bass.ds(c0, (n1 - n0) * P)]
                                 ).then_inc(E("cc_landed"), 16)

            def head_piece(i, n, j):
                load(sp, n + j, j % 4, two_blocks(j, PK * j, i * P, i * P + DM) if j < 4 else
                     one_block(j % 4, w_in, PK * (j % 4), i * 256 + (2 * DM if j < 8 else QKV)))

            def decays(d):
                sp.dma_start(dec[:].rearrange("p u c -> p (u c)"),
                             gc_dram.rearrange("r c -> (r c)")[bass.ds(d * (5 * P), 5 * P)].partition_broadcast(P)
                             ).then_inc(E("dec_landed"), 16)

            def states_in(d):
                sd = state_delta[0].rearrange("b h d e -> d h b e")
                for v in range(2):
                    sp.dma_start(s_s[:, :, v, :], sd[:, bass.ds(d * 2 + v, 1), :, :].rearrange("d h b e -> d (h b) e")
                                 ).then_inc(E("state_landed"), 16)

            def states_out(d):
                sp.wait_ge(E("sp_final"), d + 1)
                sp.wait_ge(E("ss_sum"), d * 4 + 4)
                sp.dma_start(new_sd_p[0, 0].rearrange("h d e -> d h e")[:, bass.ds(d * 2, 2), :], s_p[:]
                             ).then_inc(E("delta_out"), 16)
                sdo = new_sd_s[0].rearrange("b h d e -> d h b e")
                for v in range(2):
                    sp.dma_start(sdo[:, bass.ds(d * 2 + v, 1), :, :].rearrange("d h b e -> d (h b) e"), s_s[:, :, v, :]
                                 ).then_inc(E("delta_out"), 16)

            def cache_store(i):
                sp.wait_ge(E("cc_out"), i + 1)
                s_rows, p_rows = new_cc_s[0].rearrange("b r c -> (b r) c"), new_cc_p[0, 0]
                for n0, n1, c0 in ((0, 1, i * P), (1, 2, i * P + DM), (2, 4, i * 256 + 2 * DM)):
                    v = cc_out[:, n0:n1, :].rearrange("p n c -> p (n c)")
                    sp.dma_start(s_rows[:, bass.ds(c0, (n1 - n0) * P)], v[0:24, :]).then_inc(E("cc_dma"), 16)
                    sp.dma_start(p_rows[:, bass.ds(c0, (n1 - n0) * P)], v[24:27, :]).then_inc(E("cc_dma"), 16)

            for j in range(8):
                head_piece(0, HEADS, j)
            sp.wait_ge(E("x_lo"), KT)
            sp.wait_ge(E("ht_saved"), 16)
            cache_rows(0)
            for j in range(8, 12):
                head_piece(0, HEADS, j)
            for j in range(2):
                head_piece(1, HEADS + 12, j)
            sp.wait_ge(E("table"), 1)
            sp.wait_ge(E("delta_out"), 16)
            decays(0)
            states_in(0)
            sp.wait_ge(E("cc_t"), 1)
            cache_rows(1)
            for j in range(2, 4):
                head_piece(1, HEADS + 12, j)
            cache_store(0)
            for j in range(4, 12):
                if j == 10:
                    sp.wait_ge(E("l_mat"), 1)
                    sp.wait_ge(E("a_mat"), 1)
                    decays(1)
                head_piece(1, HEADS + 12, j)
            with sp.Fori(2, NH) as i:
                sp.wait_ge(E("cc_t"), i)
                cache_rows(i)
                for j in range(12):
                    if j == 4:
                        cache_store(i - 1)
                    if j == 5:
                        states_out(i - 2)
                    if j == 7:
                        sp.wait_ge(E("delta_out"), i * 48 - 32)
                        states_in(i - 1)
                    if j == 10:
                        sp.wait_ge(E("l_mat"), i)
                        sp.wait_ge(E("a_mat"), i)
                        decays(i)
                    head_piece(i, i * 12 + HEADS, j)

            for j in range(4):
                load(sp, OUT_A + j, j, one_block(j, w_out, PK * j, 0))
            cache_store(NH - 1)
            states_out(NH - 2)
            sp.wait_ge(E("delta_out"), 48 * (NH - 1) + 16)
            states_in(NH - 1)
            states_out(NH - 1)

        @block.gpsimd
        def _(pool):
            gp = nc.gpsimd
            for t in (ident, mask_p, tri_p, blk_s):
                gp.memset(t[:], 0.0 if t in (ident, mask_p) else 1.0).then_inc(E("consts"), 1)
            gp.memset(ones[:], 1.0).then_inc(E("consts"), 1)
            gp.memset(minushalf[:], -0.5).then_inc(E("consts"), 1)
            gp.memset(lv[:], 1.0).then_inc(E("consts"), 1)
            gp.memset(seqmask[:], 1.0).then_inc(E("consts"), 1)
            pool.wait_ge(E("consts"), 8)

            def keep_where(out, in_, base, pattern, cm, fill, op=ALU.is_ge):
                return gp.affine_select(out=out, in_=in_, compare_op=op, fill=fill, base=base, pattern=pattern,
                                        channel_multiplier=cm)

            NB = P // SLEN
            keep_where(ident[:], ident[:], 0, [[-1, P]], 1, 1.0, ALU.not_equal).then_inc(E("ident"), 1)
            keep_where(tri_p[:], tri_p[:], 0, [[1, P]], -1, 0.0).then_inc(E("consts"), 1)
            keep_where(blk_s[:], blk_s[:], 0, [[-SLEN, NB], [0, SLEN]], 1, 0.0).then_inc(E("consts"), 1)
            keep_where(mask_p[:], mask_p[:], 0, [[-1, P]], 1, NEG).then_inc(E("consts"), 1)
            pool.wait_ge(E("consts"), 11)
            keep_where(mask_s[:], mask_p[:], SLEN - 1, [[SLEN, NB], [0, SLEN]], -1, NEG).then_inc(E("consts"), 1)
            keep_where(tri_s[:], tri_p[:], 0, [[-SLEN, NB], [0, SLEN]], 1, 0.0).then_inc(E("consts"), 1)
            keep_where(blk_s[:], blk_s[:], SLEN - 1, [[SLEN, NB], [0, SLEN]], -1, 0.0).then_inc(E("consts"), 1)
            pool.wait_ge(E("ident"), 1)
            for h in range(2):
                gp.tensor_copy(shift[:, 64 * h:64 * h + 64], ident[:, 64:P]).then_inc(E("consts"), 1)
            pool.wait_ge(E("consts"), 16)
            for step, (base, pattern, cm) in enumerate(((0, [[-SLEN, NSEQ]], 1), (SLEN - 1, [[SLEN, NSEQ]], -1))):
                for h in range(2):
                    v = seqmask[64 * h:64 * h + 64, :]
                    keep_where(v, v, base, pattern, cm, 0.0).then_inc(E("consts"), 1)
                    pool.wait_ge(E("consts"), 16 + 2 * step + h + 1)
            for step in range(3):
                for k in range(LEVELS):
                    b = 1 << k
                    v = lv[:, k, :].rearrange("p (j r) -> p j r", r=2 * b)
                    n = P // (2 * b)
                    base, pattern, cm = ((-b, [[-2 * b, n], [0, 2 * b]], 1), (2 * b - 1, [[2 * b, n], [0, 2 * b]], -1),
                                         (b - 1, [[0, n], [-1, 2 * b]], 0))[step]
                    keep_where(v, v, base, pattern, cm, 0.0).then_inc(E("consts"), 1)
                pool.wait_ge(E("consts"), 20 + LEVELS * (step + 1))
            gp.tensor_copy(level[:], lv[:]).then_inc(E("c_all"), 1)
            pool.wait_ge(E("x_lo"), KT)
            pool.wait_ge(E("ht_saved"), 16)
            gp.memset(convin[:, :, 0:TAPS - 1], 0.0).then_inc(E("conv_zero"), 1)
            for e in ("pe", "act", "dve"):
                pool.wait_ge(E(f"{e}_round"), 1)
            gp.memset(ud_s[:], 0.0)
            gp.memset(p1[:], 0.0)
            gp.memset(small[:], 0.0).then_inc(E("pool_round"), 1)

            def delta(n):
                rounds(pool, n)
                pool.wait_ge(E("ident"), 1)
                for u in range(5):
                    last = gp.tensor_tensor(xm[:, u, :], ident[:], ones[:], ALU.mult)
                last.then_inc(E("x_init"), 1)
                pool.wait_ge(E("sum_sb"), n)
                gp.tensor_tensor(small[:, 8:14], small[:, 0:6], minushalf[:, 0:6], ALU.pow).then_inc(E("rnorm"), 1)
                pool.wait_ge(E("rnorm"), n)
                pool.wait_ge(E("cur"), n)
                gp.tensor_tensor(small[:, 16:20].rearrange("p (v c) -> p v c", v=2),
                                 small[:, 8:10].rearrange("p (o c) -> p o c", o=1).to_broadcast([P, 2, 2]),
                                 cur[:, EGC:EGC + 4].rearrange("p (v c) -> p v c", v=2), ALU.mult)
                gp.tensor_tensor(small[:, 20:21], small[:, 10:11], cur[:, EGC + 4:EGC + 5], ALU.mult).then_inc(E("rqe"), 1)
                pool.wait_ge(E("dec"), n)
                pool.wait_ge(E("qk_r"), n)
                for v in range(2):
                    gp.tensor_tensor(amat[:, 2 * v:2 * v + 2, :], qk_r[:, 0:2, :], dec[:, 2 * v:2 * v + 2, :], ALU.mult)
                gp.tensor_tensor(amat[:, 4, :], qk_r[:, 2, :], dec[:, 4, :], ALU.mult).then_inc(E("a_mat"), 1)
                pool.wait_ge(E("k_tok"), n)
                gp.tensor_tensor(k_m[:], k_tok[:, 2:3, :].to_broadcast([P, NSEQ, P]), wide(seqmask[:], NSEQ), ALU.mult
                                 ).then_inc(E("k_m"), 1)
                pool.wait_ge(E("ksqs_ps"), n)
                sv = s_s[:].rearrange("p b v c -> p (b v) c")
                gp.tensor_tensor(sv, sv, wide(cur[:, EGL + 4:EGL + 20], 16), ALU.mult).then_inc(E("s_scaled"), 1)
                pool.wait_ge(E("osum_sb"), n)
                gp.tensor_tensor(small[:, 32:37], small[:, 24:29], minushalf[:, 0:5], ALU.pow).then_inc(E("ro"), 1)
                pool.wait_ge(E("ro"), n)
                gp.tensor_tensor(small[:, 40:41], ones[:, 0:1], ones[:, 0:1], ALU.mult).then_inc(E("pool_round"), 1)

            with pool.Fori(1, NH) as i:
                delta(i)
            delta(NH)

        @block.scalar
        def _(act):
            sc = nc.scalar

            for k in range(0, KT, 2):
                act.wait_ge(E("tiles_t"), k + 1)
                sc.activation(ht[:, k, :], ps[:, 4 + k % 4, 0:T], ACT.Copy).then_inc(E("even_tiles"), 1)
                if k >= 4:
                    act.wait_ge(E("sq_used"), k - 3)
                act.wait_ge(E("even_tiles"), k // 2 + 1)
                sc.activation(sq[:, k % 4, :], ht[:, k, :], ACT.Square).then_inc(E("sq_even"), 1)
            act.wait_ge(E("odd_tiles"), KT // 2)
            act.dma_start(ht_dram, ht[:].rearrange("p k t -> p (k t)")).then_inc(E("ht_saved"), 16)
            act.wait_ge(E("ms"), 1)
            sc.activation(rb[:], rb[:], ACT.Sqrt).then_inc(E("rms"), 1)
            for n in range(4):
                split_hi(act, n, n, 512)
            for k in range(KT):
                act.wait_ge(E("xnorm"), k + 1)
                sc.activation(xhi[:, k, :], sq[:, k % 4, :], ACT.Copy).then_inc(E("x_hi"), 1)
            split_hi(act, HEADS, 0)
            split_hi(act, HEADS + 1, 1)
            act.wait_ge(E("gvec_in"), 32)
            sc.activation(gvec[:, 0, :], gvec[:, 0, :], ACT.Exp).then_inc(E("g_act"), 1)
            act.wait_ge(E("graw"), 1)
            sc.activation(gt[:], graw[:, :, 0:32], ACT.Tanh, scale=0.5).then_inc(E("g_act"), 1)
            act.wait_ge(E("gy"), 1)
            sc.activation(ge[:], gy[:], ACT.Abs).then_inc(E("g_act"), 1)
            act.wait_ge(E("g_act"), 3)
            sc.activation(ge[:], ge[:], ACT.Exp, scale=-1.0).then_inc(E("g_act"), 1)
            act.wait_ge(E("g_act"), 4)
            sc.activation(ge[:], ge[:], ACT.Ln, bias=1.0).then_inc(E("g_act"), 1)
            split_hi(act, HEADS + 2, 2)
            split_hi(act, HEADS + 3, 3)
            split_hi(act, HEADS + 4, 0)
            split_hi(act, HEADS + 5, 1)
            split_hi(act, HEADS + 6, 2)
            act.wait_ge(E("t_raw"), 1)
            tv = table[:, :, 0:30].rearrange("p h (t u) -> p h t u", u=5)
            sc.activation(tv[:, :, 4, :], tv[:, :, 0, :], ACT.Exp)
            sc.activation(tv[:, :, 5, :], tv[:, :, 5, :], ACT.Exp)
            sc.activation(table[:, :, EGL:EGL + 20], table[:, :, EGL:EGL + 20], ACT.Exp).then_inc(E("t_exp"), 1)
            split_hi(act, HEADS + 7, 3)
            act.wait_ge(E("gcr"), 1)
            act.dma_start(gc_dram, gcr[0:80, :]).then_inc(E("delta_out"), 16)

            def loop_of(i):
                return not isinstance(i, int)

            def qk_evac(i, used):
                act.wait_ge(E("w_used"), used)
                if loop_of(i):
                    act.wait_ge(E("conv"), i * 16)
                sc.activation(convin[:, 0:2, TAPS - 1:S_AT], ps[:, 0:2, 0:NPT], ACT.Copy)
                sc.activation(conv_strips(convin, 0, 2, TAPS - 1, SLEN), toks(ps[:, 0:2, NPT:T]), ACT.Copy
                              ).then_inc(E("qk_evac"), 1)

            def v_evac(i, used):
                act.wait_ge(E("w_used"), used)
                if loop_of(i):
                    act.wait_ge(E("conv"), i * 16)
                sc.activation(convin[:, 2:4, TAPS - 1:S_AT], ps[:, 2:4, 0:NPT], ACT.Copy)
                sc.activation(conv_strips(convin, 2, 4, TAPS - 1, SLEN), toks(ps[:, 2:4, NPT:T]), ACT.Copy
                              ).then_inc(E("v_evac"), 1)

            def z_evac(i, used):
                act.wait_ge(E("w_used"), used)
                if loop_of(i):
                    act.wait_ge(E("gate"), i)
                sc.activation(zraw[:], ps[:, 0:2, 0:T], ACT.Copy).then_inc(E("z_evac"), 1)

            def cc_evac(i):
                if loop_of(i):
                    act.wait_ge(E("conv"), i * 16)
                act.wait_ge(E("cc_t"), i + 1)
                sc.activation(conv_strips(convin, 0, 4, 0, TAPS - 1),
                              D0[:, 384:480].rearrange("p (n b r) -> p n b r", n=4, b=NSEQ), ACT.Copy
                              ).then_inc(E("cc_evac"), 1)

            def cc_tail(i):
                if loop_of(i):
                    act.wait_ge(E("cc_o"), i)
                act.wait_ge(E("qk_evac"), i + 1)
                act.wait_ge(E("v_evac"), i + 1)
                sc.activation(tail[:, :, 0:24].rearrange("p n (b r) -> p n b r", b=NSEQ),
                              conv_strips(convin, 0, 4, SLEN, TAPS - 1), ACT.Copy)
                sc.activation(tail[:, :, 24:27], convin[:, :, NPT:NPT + 3], ACT.Copy).then_inc(E("tail"), 1)

            def cc_store(i):
                if loop_of(i):
                    act.wait_ge(E("cc_dma"), i * 96)
                act.wait_ge(E("cc_o"), i + 1)
                sc.activation(cc_out[0:27, :, :], blocks(D3[0:27, :], 4), ACT.Copy).then_inc(E("cc_out"), 1)

            def halves(v, k):
                return v.rearrange("p (j h b) -> p j h b", h=2, b=1 << k)[:, :, 1, :]

            def copy_units(dst, name, samples):
                last = sc.activation(dst[:, 0:4, :], blocks(D0, 4), ACT.Copy)
                if samples:
                    last = sc.activation(dst[:, 4, :], D1[:, 0:P], ACT.Copy)
                last.then_inc(E(name), 1)

            def decays(n):
                act.wait_ge(E("diff"), n)
                sc.activation(dec[:], dec[:], ACT.Exp).then_inc(E("dec"), 1)

            def delta(n, split, cached, next_decays):
                rounds(act, n)
                act.wait_ge(E("conv"), n * 16 - 8)
                sc.activation(silu[:, 0:2, :], convout[:, 0:2, :], ACT.Tanh, scale=0.5).then_inc(E("th_qk"), 1)
                act.wait_ge(E("conv"), n * 16)
                sc.activation(silu[:, 2:4, :], convout[:, 2:4, :], ACT.Tanh, scale=0.5).then_inc(E("th_v"), 1)
                split(0)
                act.wait_ge(E("silu"), n)
                for q in range(2):
                    sc.activation(samp[:, q, :].rearrange("p (o b s) -> p o b s", o=2, b=NSEQ),
                                  sample_cols(q, q + 1).to_broadcast([P, 2, NSEQ, SLEN]), ACT.Copy)
                sc.activation(samp[:, 2, :].rearrange("p (o b s) -> p o b s", o=2, b=NSEQ), sample_cols(2, 4), ACT.Copy
                              ).then_inc(E("samp"), 1)
                split(1)
                act.wait_ge(E("kv_ps"), n)
                for q, bank in ((1, D1), (0, D0)):
                    for u in range(3):
                        last = sc.activation(sq_tok[:, q, P * u:P * u + P], bank[:, P * u:P * u + P], ACT.Square,
                                             accum_out=small[:, 54 + 3 * q + u:55 + 3 * q + u])
                last.then_inc(E("qk_sq"), 1)
                cached()
                act.wait_ge(E("z_evac"), n)
                sc.activation(gate[:], zraw[:], ACT.Tanh, scale=0.5).then_inc(E("z_tanh"), 1)
                split(2)
                act.wait_ge(E("kn_ps"), n)
                sc.activation(k_t[:], blocks(D3[:, 0:384], 3), ACT.Copy)
                sc.activation(kq_in[:, 0, :], D3[:, 256:320], ACT.Copy)
                sc.activation(kq_in[:, 1, :], samp[:, 0, 0:64], ACT.Copy).then_inc(E("k_t"), 1)
                split(3)
                act.wait_ge(E("xt"), (n - 1) * LEVELS + 1)
                copy_units(ym, "y", True)
                act.wait_ge(E("at_ps"), n)
                sc.activation(a_t[:, 0:4, :], blocks(D2, 4), ACT.Copy)
                sc.activation(a_t[:, 4, :], D3[:, 0:P], ACT.Copy).then_inc(E("a_t"), 1)
                for k in range(1, LEVELS):
                    act.wait_ge(E("lp"), (n - 1) * (LEVELS - 1) + k)
                    last = sc.activation(halves(p1[:, 0:4, :].rearrange("p u c -> p (u c)"), k), halves(D0, k), ACT.Copy)
                    if k < S_LEVELS:
                        last = sc.activation(halves(p1[:, 4, :], k), halves(D1[:, 0:P], k), ACT.Copy)
                    last.then_inc(E("p"), 1)
                    if k < 6:
                        split(3 + k)
                    act.wait_ge(E("xt"), (n - 1) * LEVELS + (k + 1))
                    copy_units(ym, "y", k < S_LEVELS)
                    if k == 4:
                        next_decays()
                    if k == 2:
                        act.wait_ge(E("ksqs_ps"), n)
                        sc.activation(ksqs[:], blocks(D3[:, 0:256], 2), ACT.Copy).then_inc(E("ksqs"), 1)
                act.wait_ge(E("u0_ps"), n)
                sc.activation(u_m[:], blocks(D1[:, 0:384], 3), ACT.Copy).then_inc(E("u0"), 1)
                act.wait_ge(E("s0_ps"), n)
                if loop_of(n):
                    act.wait_ge(E("delta_out"), n * 48 - 32)
                elif n > 1:
                    act.wait_ge(E("delta_out"), 48 * n - 32)
                sc.activation(s_p[:], blocks(D0[:, 0:256], 2), ACT.Copy).then_inc(E("s0"), 1)
                split(9)
                act.wait_ge(E("u1_ps"), n)
                sc.activation(u_m[:, 0:2, :], blocks(D2[:, 0:256], 2), ACT.Copy).then_inc(E("u1"), 1)
                split(10)
                act.wait_ge(E("o_all"), n)
                for u in range(5):
                    sc.activation(p1[:, u, :], o_m[:, u, :], ACT.Square, accum_out=small[:, 48 + u:49 + u]
                                  ).then_inc(E("osq"), 1)
                split(11)
                act.wait_ge(E("osq"), n * 5)
                sc.activation(small[:, 60:61], ones[:, 0:1], ACT.Copy).then_inc(E("act_round"), 1)

            act.wait_ge(E("x_lo"), KT)
            act.wait_ge(E("ht_saved"), 16)
            act.wait_ge(E("conv_zero"), 1)
            qk_evac(0, HEADS + 4)
            cc_evac(0)
            for j in range(8, 10):
                split_hi(act, HEADS + j, j % 4)
            v_evac(0, HEADS + 8)
            cc_tail(0)
            cc_store(0)
            for j in range(10, 12 + LEAD):
                split_hi(act, HEADS + j, j % 4)
            z_evac(0, HEADS + 12)
            act.wait_ge(E("t_exp"), 1)
            decays(1)
            sc.activation(small[:, 61:62], ones[:, 0:1], ACT.Copy).then_inc(E("act_round"), 1)

            with act.Fori(1, NH) as i:
                def split(j, i=i):
                    split_hi(act, i * 12 + (HEADS + LEAD + j), (LEAD + j) % 4)
                    if j == 3:
                        qk_evac(i, i * 12 + (HEADS + 4))
                    if j == 7:
                        v_evac(i, i * 12 + (HEADS + 8))
                        cc_tail(i)
                    if j == 9:
                        cc_store(i)

                delta(i, split, lambda i=i: cc_evac(i), lambda i=i: decays(i + 1))
                z_evac(i, i * 12 + (HEADS + 12))
            delta(NH, lambda j: None, lambda: None, lambda: None)


        @block.vector
        def _(dve):
            v = nc.vector

            for k in range(1, KT, 2):
                dve.wait_ge(E("tiles_t"), k + 1)
                v.tensor_copy(ht[:, k, :], ps[:, 4 + k % 4, 0:T]).then_inc(E("odd_tiles"), 1)
                if k >= 4:
                    dve.wait_ge(E("sq_used"), k - 3)
                dve.wait_ge(E("odd_tiles"), k // 2 + 1)
                v.tensor_tensor(sq[:, k % 4, :], ht[:, k, :], ht[:, k, :], ALU.mult).then_inc(E("sq_odd"), 1)
            dve.wait_ge(E("vecs_ps"), 1)
            v.tensor_copy(vecs[:, 0:V_SCALE], ps[:, 1, 0:V_SCALE])
            v.tensor_scalar(vecs[:, V_SCALE:V_O + 1], ps[:, 1, V_SCALE:V_O + 1], 0.5, None, ALU.mult).then_inc(E("vecs"), 1)
            cw = ps[:, 2, 0:256].rearrange("p (t n) -> p t n", t=TAPS)
            for q in range(2):
                v.tensor_copy(convw[:, :, q, :].rearrange("p h t -> p t h"), cw[:, :, NH * q:NH * q + NH])
            for q in range(2):
                last = v.tensor_copy(convw[:, :, 2 + q, :].rearrange("p h t -> p t h"),
                                     cw[:, :, 2 * NH:4 * NH].rearrange("p t (h v) -> p t h v", v=2)[:, :, :, q])
            last.then_inc(E("convw"), 1)
            dve.wait_ge(E("sq_used"), KT)
            v.tensor_scalar(rb[:], ps[:, 0, 0:T], 1.0 / DM, EPS, ALU.mult, ALU.add).then_inc(E("ms"), 1)
            dve.wait_ge(E("rms"), 1)
            v.reciprocal(rb[:], rb[:]).then_inc(E("rinv"), 1)
            dve.wait_ge(E("rinv"), 1)
            dve.wait_ge(E("vecs"), 1)

            def low_x(k):
                dve.wait_ge(E("x_hi"), k + 1)
                v.tensor_tensor(xlo[:, k, :], sq[:, k % 4, :], xhi[:, k, :].bitcast(F32), ALU.subtract
                                ).then_inc(E("x_lo"), 1)

            for k in range(KT):
                if k >= 4:
                    dve.wait_ge(E("x_lo"), k - 3)
                v.scalar_tensor_tensor(sq[:, k % 4, :], ht[:, k, :], vecs[:, k:k + 1], rb[:], ALU.mult, ALU.mult
                                       ).then_inc(E("xnorm"), 1)
                if k == 1:
                    for n in range(4):
                        split_lo(dve, n, n, 512)
                if k >= 1:
                    low_x(k - 1)
            low_x(KT - 1)
            split_lo(dve, HEADS, 0)
            split_lo(dve, HEADS + 1, 1)

            dve.wait_ge(E("w_used"), 4)
            v.tensor_copy(gfeat[:], ps[:, 3, 0:T]).then_inc(E("gfeat"), 1)
            dve.wait_ge(E("g_pe"), 1)
            gates = blocks(D0[:, 0:3 * P], 3)[:, :, 64:P]
            v.tensor_copy(graw[:, 0:2, :], gates[:, 0:2, :])
            v.tensor_copy(gtail[:], gates[:, 2, :]).then_inc(E("gtail"), 1)
            dve.wait_ge(E("g_pe"), 2)
            v.tensor_copy(graw[:, 2, :], D1[:, 0:64]).then_inc(E("graw"), 1)
            dve.wait_ge(E("graw"), 1)
            dve.wait_ge(E("gvec_in"), 32)
            v.tensor_tensor(gy[:], graw[:, :, 32:64], gvec[:, 1:2, :].to_broadcast([P, 3, 32]), ALU.add).then_inc(E("gy"), 1)
            split_lo(dve, HEADS + 2, 2)
            split_lo(dve, HEADS + 3, 3)
            dve.wait_ge(E("g_act"), 2)
            def put(col0, src):
                v.tensor_copy(table[:, :, col0:col0 + 4].rearrange("p h (v c) -> p h v c", v=2),
                              src[:, 0:2, :].rearrange("p c (h v) -> p h v c", v=2))
                for q in range(2):
                    last = v.tensor_copy(table[64 * q:64 * q + 64, :, col0 + 4],
                                         src[64 * q:64 * q + 64, 2, :].rearrange("p (h v) -> p h v", v=2)[:, :, q])
                return last

            dve.wait_ge(E("g_act"), 5)
            v.scalar_tensor_tensor(gg[:], gy[:], 0.0, ge[:], ALU.max, ALU.add).then_inc(E("g_vec"), 1)
            dve.wait_ge(E("g_vec"), 1)
            v.scalar_tensor_tensor(gg[:], gg[:], -1.0, gvec[:, 0:1, :].to_broadcast([P, 3, 32]), ALU.mult, ALU.mult
                                   ).then_inc(E("g_vec"), 1)
            dve.wait_ge(E("g_vec"), 2)
            dve.wait_ge(E("consts"), 20)
            v.tensor_tensor(gsb[0:64, :, :], gg[0:64, 2:3, :].to_broadcast([64, NSEQ, 32]),
                            seqmask[0:64, :].rearrange("p (b o) -> p b o", o=1).to_broadcast([64, NSEQ, 32]), ALU.mult
                            ).then_inc(E("gg"), 1)
            split_lo(dve, HEADS + 4, 0)
            split_lo(dve, HEADS + 5, 1)
            v.tensor_scalar(gy[:], gt[:], -0.5, -0.5, ALU.mult, ALU.add)
            v.tensor_scalar(ge[:], gt[:], 0.25, 0.25, ALU.mult, ALU.add).then_inc(E("g_vec"), 1)
            dve.wait_ge(E("g_vec"), 3)
            put(NBETA, gy)
            put(HBETA, ge)
            dve.wait_ge(E("g_pe"), 3)
            gc3, gl3 = blocks(D2[:, 0:96], 3), blocks(D2[:, 96:192], 3)
            v.tensor_copy(gcs[:], gc3).then_inc(E("g_vec"), 1)
            dve.wait_ge(E("g_vec"), 4)
            v.tensor_tensor(gt[:], gl3, gcs[:], ALU.subtract).then_inc(E("g_vec"), 1)
            put(GC, gcs)
            v.tensor_copy(table[:, :, EGL:EGL + 4].rearrange("p h (c v) -> p h c v", v=2),
                          gl3[:, 0:2, :].rearrange("p c (h v) -> p h c v", v=2))
            v.tensor_copy(table[:, :, EGL + 4:EGL + 20].rearrange("p h (b v) -> p h b v", v=2),
                          D3[:, 0:256].rearrange("p (b h v) -> p h b v", b=NSEQ, v=2))
            dve.wait_ge(E("g_vec"), 5)
            put(DEC, gt).then_inc(E("t_raw"), 1)
            dve.wait_ge(E("t_raw"), 1)
            v.tensor_scalar(blocks(gct[:], NH), table[:, :, GC:GC + 5], -1.0, None, ALU.mult).then_inc(E("gct"), 1)
            split_lo(dve, HEADS + 6, 2)
            dve.wait_ge(E("g_pe"), 4)
            v.tensor_copy(gcr[0:80, :], D1[0:80, 0:P]).then_inc(E("gcr"), 1)
            split_lo(dve, HEADS + 7, 3)
            dve.wait_ge(E("t_exp"), 1)
            v.tensor_tensor(table[:, :, NBE:NBE + 5], table[:, :, NBETA:NBETA + 5], table[:, :, EGC:EGC + 5], ALU.mult
                            ).then_inc(E("table"), 1)

            def conv_weights(i):
                v.tensor_copy(cwcur[:], convw[:, bass.ds(i, 1), :, :].rearrange("p h q t -> p (h q) t"))
                v.tensor_copy(gc_next[:], table[:, bass.ds(i, 1), GC:GC + 5].rearrange("p h c -> p (h c)")
                              ).then_inc(E("next"), 1)

            def conv(i, half, j):
                done = i * 16 + 8 * half
                if j == 0:
                    dve.wait_ge(E("next"), i + 1)
                    dve.wait_ge(E("cc_evac"), i + 1)
                    dve.wait_ge(E("v_evac" if half else "qk_evac"), i + 1)
                    dve.wait_ge(E("conv_zero"), 1)
                for q in range(2 * half, 2 * half + 2):
                    if j == 0:
                        ins = v.tensor_scalar(convout[:, q, :], convin[:, q, 0:CV], cwcur[:, q, 0:1], None, ALU.mult)
                    else:
                        dve.wait_ge(E("conv"), done + (2 * (j - 1) + q % 2 + 1))
                        ins = v.scalar_tensor_tensor(convout[:, q, :], convin[:, q, j:j + CV], cwcur[:, q, j:j + 1],
                                                     convout[:, q, :], ALU.mult, ALU.add)
                    ins.then_inc(E("conv"), 1)

            def decay_exponents(i):
                dve.wait_ge(E("dec_landed"), i * 16 + 16)
                for u in range(5):
                    last = v.scalar_tensor_tensor(dec[:, u, :], dec[:, u, :], gc_next[:, u:u + 1],
                                                  mask_p[:] if u < 4 else mask_s[:], ALU.add, ALU.add)
                last.then_inc(E("diff"), 1)

            def delta(n, d, split, conv_next, weights_next, decays_next):
                rounds(dve, n)
                dve.wait_ge(E("table"), 1)
                v.tensor_copy(cur[:], table[:, bass.ds(d, 1), :].rearrange("p h c -> p (h c)")).then_inc(E("cur"), 1)
                weights_next()
                dve.wait_ge(E("th_qk"), n)
                v.scalar_tensor_tensor(silu[:, 0:2, :], silu[:, 0:2, :], 1.0, convout[:, 0:2, :], ALU.add, ALU.mult)
                dve.wait_ge(E("th_v"), n)
                v.scalar_tensor_tensor(silu[:, 2:4, :], silu[:, 2:4, :], 1.0, convout[:, 2:4, :], ALU.add, ALU.mult
                                       ).then_inc(E("silu"), 1)
                split(0)
                split(1)
                dve.wait_ge(E("cur"), n)
                dve.wait_ge(E("kv_ps"), n)
                v.tensor_tensor(vb[:, 0:4, :], blocks(D2, 4), wide(cur[:, HBETA:HBETA + 4], 4), ALU.mult)
                dve.wait_ge(E("qk_sq"), n)
                v.tensor_scalar(small[:, 0:3], small[:, 54:57], float(P), 4 * P * EPS, ALU.mult, ALU.add)
                v.tensor_scalar(small[:, 3:6], small[:, 57:60], 4 * EPS, None, ALU.add).then_inc(E("sum_sb"), 1)
                v.tensor_scalar(vb[:, 4, :], D1[:, 384:512], cur[:, HBETA + 4:HBETA + 5], None, ALU.mult).then_inc(E("vb"), 1)
                dve.wait_ge(E("rnorm"), n)
                v.tensor_tensor(k_tok[:], blocks(D1[:, 0:384], 3), wide(small[:, 11:14], 3), ALU.mult).then_inc(E("k_tok"), 1)
                dve.wait_ge(E("z_tanh"), n)
                v.scalar_tensor_tensor(gate[:], gate[:], 1.0, zraw[:], ALU.add, ALU.mult).then_inc(E("gate"), 1)
                split(2)
                dve.wait_ge(E("kk_ps"), n)
                dve.wait_ge(E("dec"), n)
                for u in range(5):
                    last = v.scalar_tensor_tensor(lmat[:, u, :], D0[:, P * (u % 2 if u < 4 else 2):P * (u % 2 if u < 4 else 2) + P],
                                                  cur[:, NBETA + u:NBETA + u + 1], dec[:, u, :], ALU.mult, ALU.mult)
                last.then_inc(E("l_mat"), 1)
                dve.wait_ge(E("qk_ps"), n)
                v.tensor_tensor(qk_r[:], blocks(D1[:, 0:384], 3), wide(small[:, 8:11], 3), ALU.mult).then_inc(E("qk_r"), 1)
                dve.wait_ge(E("c_all"), 1)
                dve.wait_ge(E("x_init"), n)
                dve.wait_ge(E("l_mat"), n)
                v.copy_predicated(xm[:], level[:, 0:1, :].to_broadcast([P, 5, P]), lmat[:]).then_inc(E("x"), 1)
                split(3)
                for k in range(1, LEVELS):
                    dve.wait_ge(E("c_all"), 1)
                    dve.wait_ge(E(f"lx{k}"), n)
                    last = v.copy_predicated(xm[:, 0:4, :], level[:, k:k + 1, :].to_broadcast([P, 4, P]), blocks(D2, 4))
                    if k < S_LEVELS:
                        last = v.copy_predicated(xm[:, 4, :], level[:, k, :], D3[:, 0:P])
                    last.then_inc(E("x"), 1)
                    if k < 6:
                        split(3 + k)
                    if k == 3:
                        decays_next()
                    if k >= 3:
                        conv_next(0, k - 3)
                    if k == 4:
                        dve.wait_ge(E("ksqs_t"), n)
                        dve.wait_ge(E("rqe"), n)
                        v.scalar_tensor_tensor(vb[:, 4, :], D3[:, 256:384], cur[:, NBE + 4:NBE + 5], vb[:, 4, :], ALU.mult, ALU.add
                                               ).then_inc(E("r4"), 1)
                        v.tensor_scalar(o_m[:, 4, :], D3[:, 384:512], small[:, 20:21], None, ALU.mult).then_inc(E("o4"), 1)
                    if k >= 5:
                        conv_next(1, k - 5)
                dve.wait_ge(E("u0"), n)
                v.tensor_tensor(ud[:], u_m[:, 0:2, :], wide(cur[:, DEC:DEC + 4:2], 2), ALU.mult).then_inc(E("ud0"), 1)
                for q in range(2):
                    r = slice(64 * q, 64 * q + 64)
                    last = v.tensor_scalar(ud_s[r, q, :], u_m[r, 2, :], cur[r, DEC + 4:DEC + 5], None, ALU.mult)
                last.then_inc(E("ud_s"), 1)
                dve.wait_ge(E("au0_ps"), n)
                dve.wait_ge(E("o4"), n)
                v.tensor_copy(o_m[:, 0:4:2, :], blocks(D2[:, 0:256], 2))
                v.tensor_tensor(o_m[:, 4, :], D2[:, 256:384], o_m[:, 4, :], ALU.add).then_inc(E("o_c0"), 1)
                dve.wait_ge(E("ksqs1"), n)
                for q in range(2):
                    u = 2 * q + 1
                    last = v.scalar_tensor_tensor(vb[:, u, :], D1[:, P * q:P * q + P], cur[:, NBE + u:NBE + u + 1], vb[:, u, :],
                                                  ALU.mult, ALU.add)
                last.then_inc(E("r1"), 1)
                for q in range(2):
                    last = v.tensor_scalar(o_m[:, 2 * q + 1, :], D1[:, 256 + P * q:384 + P * q], small[:, 17 + 2 * q:18 + 2 * q],
                                           None, ALU.mult)
                last.then_inc(E("o1"), 1)
                split(9)
                dve.wait_ge(E("u1"), n)
                dve.wait_ge(E("s0_ps"), n)
                v.tensor_tensor(ud[:], u_m[:, 0:2, :], wide(cur[:, DEC + 1:DEC + 5:2], 2), ALU.mult).then_inc(E("ud1"), 1)
                dve.wait_ge(E("au1_ps"), n)
                dve.wait_ge(E("o1"), n)
                v.tensor_tensor(o_m[:, 1:4:2, :], blocks(D0[:, 0:256], 2), o_m[:, 1:4:2, :], ALU.add).then_inc(E("o_all"), 1)
                dve.wait_ge(E("s1_ps"), n)
                for q in range(2):
                    last = v.scalar_tensor_tensor(s_p[:, q, :], s_p[:, q, :], cur[:, EGL + 2 + q:EGL + 3 + q],
                                                  D1[:, P * q:P * q + P], ALU.mult, ALU.add)
                last.then_inc(E("sp_final"), 1)

                def states(q):
                    dve.wait_ge(E("ss_ps"), (n - 1) * 4 + (q + 1))
                    w = s_s[:, 2 * q:2 * q + 2, :, :].rearrange("p b v c -> p (b v c)")
                    v.tensor_tensor(w, (D2, D3)[q % 2], w, ALU.add).then_inc(E("ss_sum"), 1)

                dve.wait_ge(E("s_scaled"), n)
                states(0)
                states(1)
                dve.wait_ge(E("osq"), n * 5)
                v.tensor_scalar(small[:, 24:29], small[:, 48:53], 1.0 / P, EPS, ALU.mult, ALU.add).then_inc(E("osum_sb"), 1)
                conv_next(1, 2)
                states(2)
                states(3)
                split(10)
                dve.wait_ge(E("ro"), n)
                v.tensor_tensor(o_m[:], o_m[:], wide(small[:, 32:37], 5), ALU.mult).then_inc(E("on"), 1)
                split(11)
                conv_next(1, 3)
                dve.wait_ge(E("ot_ps"), n)
                b = branch[:, bass.ds(d * 2, 2), :]
                v.scalar_tensor_tensor(b[:, :, 0:NPT], blocks(D0, 2), vecs[:, V_O:V_O + 1], gate[:, :, 0:NPT], ALU.mult, ALU.mult)
                v.scalar_tensor_tensor(b[:, :, NPT:T], blocks(D1[:, 0:P], 2), vecs[:, V_O:V_O + 1], gate[:, :, NPT:T],
                                       ALU.mult, ALU.mult).then_inc(E("dve_round"), 1)

            for j in range(8, 12 + LEAD):
                split_lo(dve, HEADS + j, j % 4)
            dve.wait_ge(E("table"), 1)
            conv_weights(0)
            for half in range(2):
                for j in range(TAPS):
                    conv(0, half, j)
            decay_exponents(0)
            v.tensor_copy(small[:, 62:63], ones[:, 0:1]).then_inc(E("dve_round"), 1)
            with dve.Fori(1, NH) as i:
                delta(i, i - 1, lambda j, i=i: split_lo(dve, i * 12 + (HEADS + LEAD + j), (LEAD + j) % 4),
                      lambda half, j, i=i: conv(i, half, j), lambda i=i: conv_weights(i), lambda i=i: decay_exponents(i))
            delta(NH, NH - 1, lambda j: None, lambda half, j: None, lambda: None, lambda: None)

        @block.tensor
        def _(pe):
            mm = nc.tensor.matmul
            tr = nc.tensor.transpose

            def one(out, lhsT, rhs):
                return mm(out, lhsT, rhs, start=True, stop=True)

            pe.wait_ge(E("ident"), 1)
            pe.wait_ge(E("x_in"), 48)
            for k in range(KT):
                if k >= 4:
                    pe.wait_ge(E("odd_tiles" if k % 2 else "even_tiles"), (k - 4) // 2 + 1)
                b = ps[:, 4 + k % 4, :]
                tr(b[:, 0:P], xtok[:, 0, P * k:P * k + P], ident[:])
                tr(b[:, P:2 * P], xtok[:, 1, P * k:P * k + P], ident[:])
                tr(b[:, 2 * P:T], xtok[0:64, 2, P * k:P * k + P], ident[0:64, 0:64]).then_inc(E("tiles_t"), 1)
                if k == 3:
                    pe.wait_ge(E("rows_in"), 96)
                    tr(ps[:, 1, 0:V_O + 1], vrow[0:V_O + 1, :], ident[0:V_O + 1, 0:V_O + 1]).then_inc(E("vecs_ps"), 1)
                    for h in range(2):
                        last = tr(ps[:, 2, P * h:P * h + P], crow[:, h, :], ident[:])
                    last.then_inc(E("vecs_ps"), 1)
                if k >= 3:
                    q = k - 3
                    pe.wait_ge(E("sq_odd" if q % 2 else "sq_even"), q // 2 + 1)
                    pe.wait_ge(E("consts"), 8)
                    mm(ps[:, 0, 0:T], ones[:], sq[:, q % 4, :], start=q == 0, stop=False).then_inc(E("sq_used"), 1)
            for q in range(KT - 3, KT):
                pe.wait_ge(E("sq_odd" if q % 2 else "sq_even"), q // 2 + 1)
                mm(ps[:, 0, 0:T], ones[:], sq[:, q % 4, :], start=False, stop=q == KT - 1).then_inc(E("sq_used"), 1)
            for k in range(KT):
                if k % 4 == 0:
                    pe.wait_ge(E("w_lo"), k // 4 + 1)
                pe.wait_ge(E("x_lo"), k + 1)
                w, o = slice(P * (k % 4), P * (k % 4) + P), ps[:, 3, 0:T]
                mm(o, whi[:, k // 4, w], xhi[:, k, :], start=k == 0, stop=False)
                mm(o, whi[:, k // 4, w], xlo[:, k, :], start=False, stop=False)
                last = mm(o, wlo[:, k // 4, w], xhi[:, k, :], start=False, stop=k == KT - 1)
                if k % 4 == 3:
                    last.then_inc(E("w_used"), 1)
            pe.wait_ge(E("gfeat"), 1)
            for q, c0 in enumerate((0, P, T - P)):
                last = tr(D0[:, P * q:P * q + P], gfeat[:, c0:c0 + P], ident[:])
            last.then_inc(E("g_pe"), 1)
            pe.wait_ge(E("w_used"), 4)
            pe.wait_ge(E("vecs"), 1)
            pe.wait_ge(E("convw"), 1)
            pe.wait_ge(E("ms"), 1)

            def project(i, at, count):
                for p in range(at, at + count):
                    job, k = p // KT, p % KT
                    n = i * 12 + (HEADS + p // PK)
                    if k == 0 and not isinstance(i, int):
                        pe.wait_ge(E(("z_evac", "v_evac", "qk_evac")[job]), i if job < 2 else i + 1)
                    if k == 0 and isinstance(i, int) and job == 2:
                        pe.wait_ge(E("qk_evac"), 1)
                    if k % PK == 0:
                        pe.wait_ge(E("w_lo"), n + 1)
                    last = k_tile((p // PK) % 4, k % PK, xhi, xlo, k, job % 2, k == 0, k == KT - 1)
                    if k % PK == PK - 1:
                        last.then_inc(E("w_used"), 1)

            def cache_in(i):
                for q in range(4):
                    last = tr(D0[:, 384 + 24 * q:408 + 24 * q], cc_in[0:24, q, :], ident[0:24, 0:24])
                last.then_inc(E("cc_t"), 1)

            def cache_out(i):
                pe.wait_ge(E("tail"), i + 1)
                pe.wait_ge(E("ident"), 1)
                for q in range(4):
                    last = tr(D3[0:27, P * q:P * q + P], tail[:, q, :], ident[:])
                last.then_inc(E("cc_o"), 1)

            pe.wait_ge(E("gtail"), 1)
            pe.wait_ge(E("consts"), 16)
            one(D1[:, 0:64], shift[:], gtail[:]).then_inc(E("g_pe"), 1)
            project(0, 0, 16)
            pe.wait_ge(E("gg"), 1)
            for q in range(3):
                one(D2[:, 32 * q:32 * q + 32], (tri_p if q < 2 else tri_s)[:], gg[:, q, :])
            for q in range(3):
                one(D2[:, 96 + 32 * q:128 + 32 * q], (ones if q < 2 else blk_s)[:], gg[:, q, :])
            one(D3[:, 0:256], ones[0:64, :], gsb[0:64, :, :].rearrange("p b h -> p (b h)")).then_inc(E("g_pe"), 1)
            project(0, 16, 8)
            pe.wait_ge(E("gct"), 1)
            tr(D1[0:80, 0:P], gct[:], ident[:]).then_inc(E("g_pe"), 1)
            pe.wait_ge(E("t_raw"), 1)
            pe.wait_ge(E("cc_landed"), 48)
            cache_in(0)
            project(0, 24, 12)
            pe.wait_ge(E("cc_evac"), 1)
            cache_out(0)
            project(0, 36, 12)
            pe.wait_ge(E("gcr"), 1)
            pe.wait_ge(E("cc_out"), 1)
            one(D2[:, 0:1], ident[:], ones[:, 0:1]).then_inc(E("pe_round"), 1)

            def delta(n, fill, cached_landed, cached_in, cached_out, cached_gone):
                fill(9)
                rounds(pe, n)
                cached_landed()
                pe.wait_ge(E("samp"), n)
                tr(D0[:, 0:P], silu[:, 0, 0:P], ident[:])
                tr(D0[:, P:2 * P], silu[:, 0, P:2 * P], ident[:])
                tr(D0[:, 2 * P:3 * P], samp[:, 0, :], ident[:])
                cached_in()
                tr(D1[:, 0:P], silu[:, 1, 0:P], ident[:])
                tr(D1[:, P:2 * P], silu[:, 1, P:2 * P], ident[:])
                tr(D1[:, 2 * P:3 * P], samp[:, 1, :], ident[:])
                tr(D1[:, 3 * P:4 * P], samp[:, 2, :], ident[:])
                for u in range(4):
                    last = tr(D2[:, P * u:P * u + P], silu[:, 2 + u // 2, P * (u % 2):P * (u % 2) + P], ident[:])
                last.then_inc(E("kv_ps"), 1)
                fill(5)
                pe.wait_ge(E("k_tok"), n)
                for u in range(3):
                    last = tr(D3[:, P * u:P * u + P], k_tok[:, u, :], ident[:])
                last.then_inc(E("kn_ps"), 1)
                fill(1)
                pe.wait_ge(E("k_t"), n)
                pe.wait_ge(E("sum_sb"), n)
                for u in range(3):
                    last = one(D0[:, P * u:P * u + P], k_t[:, u, :], k_t[:, u, :])
                last.then_inc(E("kk_ps"), 1)
                pe.wait_ge(E("vb"), n)
                for u in range(3):
                    q = silu[:, 0, P * u:P * u + P] if u < 2 else samp[:, 0, :]
                    last = one(D1[:, P * u:P * u + P], q, k_t[:, u, :])
                last.then_inc(E("qk_ps"), 1)
                fill(3)

                def units(dst0, dst1, lhs, rhs, name, samples):
                    for u in range(5 if samples else 4):
                        o = dst0[:, P * u:P * u + P] if u < 4 else dst1[:, 0:P]
                        last = one(o, lhs[:, u, :], rhs[:, u, :])
                    last.then_inc(E(name), 1)

                def upper(v, k):
                    return v.rearrange("p (j h b) -> p j h b", h=2, b=1 << k)[:, :, 1, :]

                def turned(dst0, dst1, src, name, samples):
                    for u in range(5 if samples else 4):
                        o = dst0[:, P * u:P * u + P] if u < 4 else dst1[:, 0:P]
                        last = tr(o, src[:, u, :], ident[:])
                    last.then_inc(E(name), 1)

                pe.wait_ge(E("x"), (n - 1) * LEVELS + 1)
                turned(D0, D1, xm, "xt", True)
                fill(1)
                pe.wait_ge(E("a_mat"), n)
                turned(D2, D3, amat, "at_ps", True)
                for k in range(1, LEVELS):
                    s = k < S_LEVELS
                    pe.wait_ge(E("y"), (n - 1) * LEVELS + k)
                    for u in range(5 if s else 4):
                        o = D0[:, P * u:P * u + P] if u < 4 else D1[:, 0:P]
                        last = one(upper(o, k), lmat[:, u, :], upper(ym[:, u, :], k))
                    last.then_inc(E("lp"), 1)
                    fill(1)
                    pe.wait_ge(E("p"), (n - 1) * (LEVELS - 1) + k)
                    if k == 1:
                        pe.wait_ge(E("a_t"), n)
                    units(D2, D3, p1, xm, f"lx{k}", s)
                    fill(2 if k == 1 else 1)
                    pe.wait_ge(E("x"), (n - 1) * LEVELS + (k + 1))
                    turned(D0, D1, xm, "xt", s)
                    if k == 2:
                        pe.wait_ge(E("state_landed"), n * 32)
                        pe.wait_ge(E("x"), (n - 1) * LEVELS + 3)
                        for b in range(NSEQ):
                            if b in (3, 6):
                                fill(1)
                            for q in range(2):
                                o = D3[:, 0:256].rearrange("p (m v b s) -> p m v b s", m=2, v=2, b=NSEQ)[:, :, q, b, :]
                                last = one(o, s_s[:, b, q, :], kq_in[:, :, SLEN * b:SLEN * b + SLEN])
                        last.then_inc(E("ksqs_ps"), 1)
                    if k == 3:
                        pe.wait_ge(E("ksqs"), n)
                        for q in range(2):
                            last = tr(D3[:, 256 + P * q:384 + P * q], ksqs[:, q, :], ident[:])
                        last.then_inc(E("ksqs_t"), 1)
                    fill(1)
                pe.wait_ge(E("y"), n * LEVELS)
                pe.wait_ge(E("r4"), n)
                for q, u in enumerate((0, 2, 4)):
                    last = one(D1[:, P * q:P * q + P], ym[:, u, :], vb[:, u, :])
                last.then_inc(E("u0_ps"), 1)
                fill(1)
                pe.wait_ge(E("u0"), n)
                for q, u in enumerate((0, 2, 4)):
                    last = one(D2[:, P * q:P * q + P], a_t[:, u, :], u_m[:, q, :])
                last.then_inc(E("au0_ps"), 1)
                pe.wait_ge(E("ud0"), n)
                one(D0[:, 0:256], k_tok[:, 0, :], ud[:].rearrange("p v c -> p (v c)")).then_inc(E("s0_ps"), 1)
                fill(1)
                pe.wait_ge(E("s0"), n)
                sp2 = s_p[:].rearrange("p v c -> p (v c)")
                one(D1[:, 0:256], k_t[:, 1, :], sp2)
                one(D1[:, 256:512], silu[:, 0, P:2 * P], sp2).then_inc(E("ksqs1"), 1)
                cached_out()
                fill(1)
                pe.wait_ge(E("r1"), n)
                pe.wait_ge(E("o_c0"), n)
                for q, u in enumerate((1, 3)):
                    last = one(D2[:, P * q:P * q + P], ym[:, u, :], vb[:, u, :])
                last.then_inc(E("u1_ps"), 1)
                fill(1)
                pe.wait_ge(E("u1"), n)
                for q, u in enumerate((1, 3)):
                    last = one(D0[:, P * q:P * q + P], a_t[:, u, :], u_m[:, q, :])
                last.then_inc(E("au1_ps"), 1)
                pe.wait_ge(E("ud1"), n)
                pe.wait_ge(E("o1"), n)
                one(D1[:, 0:256], k_tok[:, 1, :], ud[:].rearrange("p v c -> p (v c)")).then_inc(E("s1_ps"), 1)
                pe.wait_ge(E("k_m"), n)
                pe.wait_ge(E("ud_s"), n)
                for q in range(4):
                    if q >= 2:
                        if q == 2:
                            fill(1)
                        pe.wait_ge(E("ss_sum"), (n - 1) * 4 + (q - 1))
                    bank = (D2, D3)[q % 2]
                    if q == 1:
                        cached_gone()
                    for b in range(2):
                        last = one(bank[:, 256 * b:256 * b + 256], k_m[:, 2 * q + b, :], ud_s[:].rearrange("p v c -> p (v c)"))
                    last.then_inc(E("ss_ps"), 1)
                fill(3)
                pe.wait_ge(E("on"), n)
                pe.wait_ge(E("sp_final"), n)
                turned(D0, D1, o_m, "ot_ps", True)
                one(D2[:, 0:1], ident[:], ones[:, 0:1]).then_inc(E("pe_round"), 1)
                fill(None)

            def beside(i):
                at = [0]

                def fill(count):
                    count = 48 - at[0] if count is None else count
                    project(i, at[0], count)
                    at[0] += count
                return fill

            with pe.Fori(1, NH) as i:
                fill = beside(i)

                def cached_landed(i=i):
                    pe.wait_ge(E("cc_landed"), i * 48 + 48)

                def cached_in(i=i):
                    cache_in(i)

                def cached_out(i=i):
                    pe.wait_ge(E("cc_evac"), i + 1)
                    cache_out(i)

                def cached_gone(i=i):
                    pe.wait_ge(E("cc_out"), i + 1)
                delta(i, fill, cached_landed, cached_in, cached_out, cached_gone)
            delta(NH, lambda count: None, lambda: None, lambda: None, lambda: None, lambda: None)

    def norm_act(act, r, tiles):
        act.wait_ge(E("ms"), r + 1)
        nc.scalar.activation(rb2[:], rb2[:], ACT.Sqrt).then_inc(E("rms"), 1)
        for k in range(tiles):
            act.wait_ge(E("xnorm"), KT * r + k + 1)
            nc.scalar.activation(xhi[:, k, :], xn[:, k % 4, :], ACT.Copy).then_inc(E("x_hi"), 1)

    def norm_scale(dve, r):
        dve.wait_ge(E("ssum"), 10 * r)
        nc.vector.tensor_scalar(rb2[:], D0[:, 0:T], 1.0 / DM, EPS, ALU.mult, ALU.add).then_inc(E("ms"), 1)
        dve.wait_ge(E("rms"), r + 1)
        nc.vector.reciprocal(rb2[:], rb2[:]).then_inc(E("rinv"), 1)
        dve.wait_ge(E("rinv"), r + 1)

    def norm_tile(dve, r, k):
        nc.vector.scalar_tensor_tensor(xn[:, k % 4, :], ht[:, k, :], vecs[:, KT * r + k:KT * r + k + 1], rb2[:],
                                       ALU.mult, ALU.mult).then_inc(E("xnorm"), 1)

    def output_projection(first, w3, job0, r):
        last_phase = r == 2
        split_base = 8 * (r - 1)
        with nc.Block() as block:
            @block.sync
            def _(sp):
                if r == 1:
                    sp.wait_ge(E("ht_saved"), 16)
                    sp.dma_start(ht[:].rearrange("p k t -> p (k t)"), ht_dram).then_inc(E("ht_in"), 16)
                for half in range(2):
                    with sp.Fori(1 - half, 8) as j:
                        for pc in range(4):
                            load(sp, j * 4 + (first + 32 * half + pc), pc, one_block(pc, w3, KT * half + PK * pc, j * 256))
                if not last_phase:
                    sp.wait_ge(E("cc_dma"), 96 * NH)
                    sp.wait_ge(E("delta_out"), 48 * NH + 16)
                    for pc in range(4):
                        load(sp, first + 64 + pc, pc, one_block(pc, pw_in, PK * pc, 0))
                if last_phase:
                    for ch in range(4):
                        c = slice(512 * ch, 512 * ch + 512)
                        sp.wait_ge(E("y_tiles"), 4 * ch + 4)
                        for g_ in range(2):
                            sp.dma_start(y_prompt[0, P * g_:P * g_ + P, c], ytok[:, g_, c]).then_inc(E("rows_out"), 16)
                        sp.dma_start(y_sample.rearrange("b s c -> (b s) c")[:, c], ytok[0:64, 2, c]).then_inc(E("rows_out"), 16)
                    sp.wait_ge(E("rows_out"), 12 * 16)
                    sp.wait_ge(E("cc_dma"), 96 * NH)
                    sp.wait_ge(E("delta_out"), 48 * NH + 16)
                    sp.wait_ge(E("cp_dma"), 32 * NH + 16)

            @block.gpsimd
            def _(pool):
                nc.gpsimd.memset(sqp[:, 1, :, :], 0.0).then_inc(E("sqp"), 1)

            @block.scalar
            def _(act):
                sc = nc.scalar
                for half in range(2):
                    for ch in range(4):
                        if ch == 0:
                            act.wait_ge(E("w_used"), first + 32 * half)
                        k0 = KT * half + 4 * ch
                        sc.activation(xhi[:, 4 * ch:4 * ch + 4, :], branch[:, k0:k0 + 4, :], ACT.Copy).then_inc(E("b_hi"), 1)
                    clipped = last_phase and half == 1

                    def splits(j, count, half=half):
                        for pc in range(count):
                            split_hi(act, j * 4 + (first + 32 * half + LEAD + pc), (LEAD + pc) % 4)

                    def square(i, jb):
                        act.wait_ge(E(f"free{jb}"), i + (job0 + 8) // 2 + 2)
                        act.wait_ge(E("ssum"), i * 2 + (10 * (r - 1) + jb + 1))
                        sc.activation(sqp[:, jb, :, :], ht[:, bass.ds(i * 4 + 2 * jb, 2), :], ACT.Square).then_inc(E("sqp"), 1)

                    with act.Fori(0, 3 if clipped else 4) as i:
                        for jb in range(2):
                            splits(i * 2 + jb, 4)
                            if half == 1:
                                square(i, jb)
                    if clipped:
                        splits(6, 4)
                        square(3, 0)
                        splits(7, 2)
                        square(3, 1)
                if last_phase:
                    norm_act(act, r, 0)
                if last_phase:
                    for k in range(KT):
                        act.wait_ge(E("tiles_t"), KT + k + 1)
                        sc.activation(ytok[:, 0:2, P * k:P * k + P], blocks(ps[:, k % 4, 0:256], 2), ACT.Copy)
                        sc.activation(ytok[0:64, 2, P * k:P * k + P], ps[0:64, k % 4, 256:384], ACT.Copy
                                      ).then_inc(E("y_tiles"), 1)

            @block.vector
            def _(dve):
                v = nc.vector
                if r == 1:
                    for pair in range(2):
                        v.tensor_copy(small[:, pair:pair + 1], ones[:, 0:1]).then_inc(E(f"free{pair}"), 1)
                for half in range(2):
                    for ch in range(4):
                        k0 = KT * half + 4 * ch
                        dve.wait_ge(E("b_hi"), split_base + 4 * half + ch + 1)
                        v.tensor_tensor(xlo[:, 4 * ch:4 * ch + 4, :], branch[:, k0:k0 + 4, :],
                                        xhi[:, 4 * ch:4 * ch + 4, :].bitcast(F32), ALU.subtract).then_inc(E("b_lo"), 1)
                    clipped = last_phase and half == 1

                    def job(i, jb, count, half=half):
                        for pc in range(count):
                            split_lo(dve, i * 8 + (first + 32 * half + 4 * jb + LEAD + pc), (LEAD + pc) % 4)
                        if half == 1:
                            dve.wait_ge(E(f"free{jb}"), i + (job0 // 2 + 2))
                        dve.wait_ge(E("w_used"), i * 8 + (first + 32 * half + 4 * jb + 4))
                        dve.wait_ge(E("ht_in"), 16)
                        tiles = ht[:, bass.ds(i * 4 + 2 * jb, 2), :]
                        v.tensor_tensor(tiles, ps[:, 2 * jb:2 * jb + 2, 0:T], tiles, ALU.add).then_inc(E(f"free{jb}"), 1)

                    with dve.Fori(0, 3 if clipped else 4) as i:
                        for jb in range(2):
                            job(i, jb, 4)
                    if clipped:
                        job(3, 0, 4)
                        job(3, 1, 2)
                if last_phase:
                    norm_scale(dve, r)
                    for k in range(KT):
                        if k >= 4:
                            dve.wait_ge(E("tiles_t"), KT + k - 3)
                        norm_tile(dve, r, k)

            @block.tensor
            def _(pe):
                mm = nc.tensor.matmul

                def add_squares(jb, i, stop=False):
                    pe.wait_ge(E("sqp"), i * 2 + (9 * (r - 1) + 1 + jb))
                    mm(D0[:, 0:T], ones[:], sqp[:, 1 - jb, 0, :], start=False, stop=False)
                    mm(D0[:, 0:T], ones[:], sqp[:, 1 - jb, 1, :], start=False, stop=stop).then_inc(E("ssum"), 1)

                pe.wait_ge(E("sqp"), 9 * (r - 1) + 1)
                mm(D0[:, 0:T], ones[:], sqp[:, 1, 0, :], start=True, stop=False).then_inc(E("ssum"), 1)
                for half in range(2):
                    with pe.Fori(0, 4) as i:
                        for jb in range(2):
                            pe.wait_ge(E(f"free{jb}"), i + (job0 // 2 + 4 * half + 1))
                            for pc in range(4):
                                pe.wait_ge(E("w_lo"), i * 8 + (first + 32 * half + 4 * jb + pc + 1))
                                pe.wait_ge(E("b_lo"), split_base + 4 * half + pc + 1)
                                for k in range(4):
                                    last = k_tile(pc, k, xhi, xlo, 4 * pc + k, jb, pc + k == 0, pc + k == 6)
                                last.then_inc(E("w_used"), 1)
                            if half == 1:
                                add_squares(jb, i)
                add_squares(0, 4, True)
                if last_phase:
                    for k in range(KT):
                        pe.wait_ge(E("xnorm"), KT * r + k + 1)
                        if k >= 4:
                            pe.wait_ge(E("y_tiles"), k - 3)
                        b = ps[:, k % 4, :]
                        x = xn[:, k % 4, :]
                        nc.tensor.transpose(b[:, 0:P], x[:, 0:P], ident[:])
                        nc.tensor.transpose(b[:, P:2 * P], x[:, P:2 * P], ident[:])
                        nc.tensor.transpose(b[0:64, 2 * P:3 * P], x[:, 2 * P:T], ident[:]).then_inc(E("tiles_t"), 1)

    output_projection(OUT_A, w_out, 0, 1)

    with nc.Block() as block:
        def z_cols(gi, t):
            return t * 256 + (1024 * gi + DI)

        @block.sync
        def _(sp):
            sp.dma_start(new_cp_s[0, :, 0:PB - SLEN, :], cache_pool[0, :, SLEN:PB, :]).then_inc(E("cp_dma"), 16)
            cp = cache_pool[0].rearrange("b r c -> (b r) c")
            for gi in range(NG):
                base = POOL + 40 * gi
                wg = pool_w_group[0, gi].rearrange("(k p) c -> p k c", p=P)

                def cached_and_z(t):
                    sp.wait_ge(E("cp_t"), t + (4 * gi + 1))
                    sp.dma_start(cp_in[0:NSEQ * PB, :], cp[:, bass.ds(t * 256 + 1024 * gi, 256)]).then_inc(E("cp_landed"), 16)
                    for pc in range(4):
                        load(sp, t * 8 + (base + 4 + pc), pc, one_block(pc, pw_in, PK * pc, z_cols(gi, t)))

                with sp.Fori(0, 3) as t:
                    cached_and_z(t)
                    for pc in range(4):
                        load(sp, t * 8 + (base + 8 + pc), pc, one_block(pc, pw_in, PK * pc, t * 256 + (1024 * gi + 256)))
                cached_and_z(3)
                for q in range(8):
                    load(sp, base + 32 + q, q % 4, one_block(q % 4, wg, PK * (q % 2), 256 * (q // 2)))
                for pc in range(4):
                    c1 = 1024 * (gi + 1) if gi + 1 < NG else 0
                    load(sp, base + 40 + pc, pc, one_block(pc, pw_in if gi + 1 < NG else pw_out, PK * pc, c1))

        @block.gpsimd
        def _(pool):
            gp = nc.gpsimd
            gp.memset(ubuf[:, :, 0:PB], 0.0).then_inc(E("pool_zero"), 1)
            for gi, win in enumerate(WINDOWS):
                for t in range(PB):
                    gp.memset(rcount[:, gi, t:t + 1], 1.0 / min(t + 1, win))
            gp.memset(rcount[:, :, PB:PB + 1], 1.0).then_inc(E("rcount"), 1)

        @block.scalar
        def _(act):
            sc = nc.scalar
            norm_act(act, 1, KT)
            for c, name in enumerate(("ptail", "cp_out")):
                sc.activation(small[:, 8 + c:9 + c], ones[:, 0:1], ACT.Copy).then_inc(E(name), 1)
            for gi in range(NG):
                base, g4 = POOL + 40 * gi, 4 * gi

                def split(t, q):
                    split_hi(act, t * 8 + (base + LEAD + q), (LEAD + q) % 4)

                with act.Fori(0, 4) as t:
                    for q in range(3):
                        split(t, q)
                    act.wait_ge(E("pooled"), t + (g4 + 1))
                    act.wait_ge(E("cp_t"), t + (g4 + 2))
                    sc.activation(pool_strips(ubuf, 0, PB), blocks(D1[:, 0:256], 2)[:, :, 0:NSEQ * PB].rearrange(
                        "p n (b r) -> p n b r", b=NSEQ), ACT.Copy)
                    split(t, 3)
                    act.wait_ge(E("w_used"), t * 8 + (base + 4))
                    sc.activation(ubuf[:, :, PB:PS_AT], ps[:, 0:2, 0:NPT], ACT.Copy)
                    sc.activation(pool_strips(ubuf, PB, SLEN), toks(ps[:, 0:2, NPT:T]), ACT.Copy).then_inc(E("free0"), 1)
                    act.wait_ge(E("free0"), t + (J_POOL // 2 + 6 * gi + 2))
                    act.wait_ge(E("cp_o"), t + (g4 + 1))
                    sc.activation(toks(ptail[:, :, 0:64]), pool_strips(ubuf, PB, SLEN), ACT.Copy)
                    sc.activation(ptail[:, :, 64:79], ubuf[:, :, NPT:NPT + PB], ACT.Copy).then_inc(E("ptail"), 1)
                    split(t, 4)
                    split(t, 5)
                    act.wait_ge(E("pooled"), t + (g4 + 2))
                    act.wait_ge(E("w_used"), base)
                    sc.activation(phi[:, bass.ds(t * 2, 2), :], pooled[:], ACT.Copy).then_inc(E("p_hi"), 1)
                    act.wait_ge(E("cp_o"), t + (g4 + 2))
                    act.wait_ge(E("cp_dma"), t * 32 + (32 * g4 + 16))
                    sc.activation(cp_out[0:79, :], D2[0:79, 0:256], ACT.Copy).then_inc(E("cp_out"), 1)
                    act.wait_ge(E("cp_out"), t + (g4 + 2))
                    c = bass.ds(t * 256 + 1024 * gi, 256)
                    act.dma_start(new_cp_s[0, :, PB - SLEN:PB, c], cp_out[0:64, :]).then_inc(E("cp_dma"), 16)
                    act.dma_start(new_cp_p[0, 0, :, c], cp_out[64:79, :]).then_inc(E("cp_dma"), 16)
                    split(t, 6)
                    split(t, 7)
                    act.wait_ge(E("w_used"), t * 8 + (base + 8))
                    act.wait_ge(E("s2z"), t + (g4 + 1))
                    sc.activation(ztanh[:], ps[:, 2:4, 0:T], ACT.Tanh, scale=0.5).then_inc(E("ztanh"), 1)
                for q in range(8):
                    split(4, q)

        @block.vector
        def _(dve):
            v = nc.vector
            norm_scale(dve, 1)
            for k in range(KT + 1):
                if k < KT:
                    if k >= 4:
                        dve.wait_ge(E("x_lo"), KT + k - 3)
                    norm_tile(dve, 1, k)
                if k >= 1:
                    dve.wait_ge(E("x_hi"), KT + k)
                    v.tensor_tensor(xlo[:, k - 1, :], xn[:, (k - 1) % 4, :], xhi[:, k - 1, :].bitcast(F32), ALU.subtract
                                    ).then_inc(E("x_lo"), 1)
            for c, name in enumerate(("pooled", "s2z", "p_lo")):
                v.tensor_copy(small[:, 1 + c:2 + c], ones[:, 0:1]).then_inc(E(name), 1)
            for gi, win in enumerate(WINDOWS):
                base, g4 = POOL + 40 * gi, 4 * gi
                adds = gi + 1

                def split(t, q):
                    split_lo(dve, t * 8 + (base + LEAD + q), (LEAD + q) % 4)

                def sums_before(k):
                    return k * (k + 1) // 2 * 4

                with dve.Fori(0, 4) as t:
                    for q in range(4):
                        split(t, q)
                    dve.wait_ge(E("free0"), t + (J_POOL // 2 + 6 * gi + 2))
                    dve.wait_ge(E("pool_zero"), 1)
                    src, at = ubuf, t * adds + sums_before(gi)
                    for a in range(adds):
                        n = PW - (2 << a) + 1
                        dst = (ws_a, ws_b)[a % 2]
                        if a:
                            dve.wait_ge(E("wsum"), t * adds + (sums_before(gi) + a))
                        v.tensor_tensor(dst[:, :, 0:n], src[:, :, 0:n], src[:, :, (1 << a):(1 << a) + n], ALU.add
                                        ).then_inc(E("wsum"), 1)
                        src = dst
                        if a == 0:
                            split(t, 4)
                    dve.wait_ge(E("p_lo"), t + (g4 + 1))
                    dve.wait_ge(E("rcount"), 1)
                    dve.wait_ge(E("wsum"), t * adds + (sums_before(gi) + adds))
                    o = PB + 1 - win
                    v.scalar_tensor_tensor(pooled[:, :, PB:NPT], src[:, :, o + PB:o + NPT], 1.0 / win, ubuf[:, :, 2 * PB:PS_AT],
                                           ALU.mult, ALU.subtract)
                    for h in range(2):
                        v.scalar_tensor_tensor(toks(pooled[:, h:h + 1, NPT:T])[:, 0], pool_strips(src, o, SLEN)[:, h], 1.0 / win,
                                               pool_strips(ubuf, PB, SLEN)[:, h], ALU.mult, ALU.subtract)
                    v.tensor_tensor(pooled[:, :, 0:PB], src[:, :, o:o + PB], rcount[:, gi:gi + 1, 0:PB].to_broadcast([P, 2, PB]),
                                    ALU.mult).then_inc(E("pfirst"), 1)
                    dve.wait_ge(E("pfirst"), t + (g4 + 1))
                    v.tensor_tensor(pooled[:, :, 0:PB], pooled[:, :, 0:PB], ubuf[:, :, PB:2 * PB], ALU.subtract
                                    ).then_inc(E("pooled"), 1)
                    split(t, 5)
                    dve.wait_ge(E("p_hi"), t + (g4 + 1))
                    v.tensor_tensor(plo[:, bass.ds(t * 2, 2), :], pooled[:], phi[:, bass.ds(t * 2, 2), :].bitcast(F32),
                                    ALU.subtract).then_inc(E("p_lo"), 1)
                    split(t, 6)
                    split(t, 7)
                    dve.wait_ge(E("ztanh"), t + (g4 + 1))
                    v.scalar_tensor_tensor(s2z[:, bass.ds(t * 2, 2), :], ztanh[:], 1.0, ps[:, 2:4, 0:T], ALU.add, ALU.mult
                                           ).then_inc(E("s2z"), 1)
                    dve.wait_ge(E("s2z"), t + (g4 + 2))
                    v.tensor_copy(small[:, 0:1], ones[:, 0:1]).then_inc(E("free1"), 1)
                for jb in range(4):
                    split(4, 2 * jb)
                    split(4, 2 * jb + 1)
                    dve.wait_ge(E("w_used"), base + 32 + 2 * jb + 2)
                    for h in range(2):
                        k = 8 * gi + 2 * jb + h
                        last = v.scalar_tensor_tensor(branch[:, k, :], ps[:, 2 * (jb % 2) + h, 0:T],
                                                      vecs[:, V_SCALE + k:V_SCALE + k + 1], s2z[:, 2 * jb + h, :],
                                                      ALU.mult, ALU.mult)
                    last.then_inc(E(f"free{jb % 2}"), 1)

        @block.tensor
        def _(pe):
            for c, name in enumerate(("cp_t", "cp_o")):
                nc.tensor.matmul(D3[:, c:c + 1], ident[:], ones[:, 0:1], start=True, stop=True).then_inc(E(name), 1)
            for gi in range(NG):
                base, g4, job = POOL + 40 * gi, 4 * gi, J_POOL // 2 + 6 * gi

                def pieces(t, q, count, pair):
                    for pc in range(q, q + count):
                        pe.wait_ge(E("w_lo"), t * 8 + (base + pc + 1))
                        if gi == 0:
                            pe.wait_ge(E("x_lo"), KT + 4 * (pc % 4) + 4)
                        for k in range(4):
                            kk = 4 * (pc % 4) + k
                            last = k_tile(pc % 4, k, xhi, xlo, kk, pair, kk == 0, kk == KT - 1)
                        last.then_inc(E("w_used"), 1)

                with pe.Fori(0, 4) as t:
                    pe.wait_ge(E("free0"), t + (job + 1))
                    pieces(t, 0, 2, 0)
                    pe.wait_ge(E("cp_landed"), t * 16 + (64 * gi + 16))
                    pe.wait_ge(E("ptail"), t + (g4 + 1))
                    for h in range(2):
                        last = nc.tensor.transpose(D1[:, P * h:P * h + NSEQ * PB], cp_in[0:NSEQ * PB, P * h:P * h + P],
                                                   ident[0:NSEQ * PB, 0:NSEQ * PB])
                    last.then_inc(E("cp_t"), 1)
                    pieces(t, 2, 2, 0)
                    pe.wait_ge(E("free1"), t + (job + 1))
                    pieces(t, 4, 2, 1)
                    pe.wait_ge(E("ptail"), t + (g4 + 2))
                    pe.wait_ge(E("cp_out"), t + (g4 + 1))
                    for h in range(2):
                        last = nc.tensor.transpose(D2[0:79, P * h:P * h + P], ptail[:, h, :], ident[:])
                    last.then_inc(E("cp_o"), 1)
                    pieces(t, 6, 2, 1)
                pe.wait_ge(E("p_lo"), g4 + 5)
                for jb in range(4):
                    pe.wait_ge(E(f"free{jb % 2}"), job + 4 + jb // 2 + 1)
                    for pc in range(2):
                        pe.wait_ge(E("w_lo"), base + 32 + 2 * jb + pc + 1)
                        for k in range(4):
                            kk = 4 * pc + k
                            last = k_tile((2 * jb + pc) % 4, k, phi, plo, kk, jb % 2, kk == 0, kk == 7)
                        last.then_inc(E("w_used"), 1)

    output_projection(OUT_B, pw_out, J_OUT_B, 2)


_INS = ("x_prompt", "x_sample", "state_delta", "cache_conv", "cache_pool", "norm_w", "final_norm_w", "delta_w_in",
        "delta_conv_w", "delta_a_log", "delta_dt_bias", "delta_o_norm_w", "delta_w_out", "pool_w_in", "pool_w_group",
        "pool_scale", "pool_w_out")
_OUTS = ((1, NPT, DM), (NSEQ, SLEN, DM), (1, 1, 2 * NH, P, P), (1, 1, TAPS - 1, QKV), (1, 1, PB, DI),
         (1, NSEQ, 2 * NH, P, P), (1, NSEQ, TAPS - 1, QKV), (1, NSEQ, PB, DI))


def kernel(**inputs):
    import numpy as _np
    import concourse.bacc as _bacc
    from concourse import mybir as _mybir
    from concourse.bass_utils import run_bass_kernel_spmd as _run

    nc = _bacc.Bacc("TRN2", target_bir_lowering=False, num_devices=1)
    arrays, args = {}, []
    for name in _INS:
        a = _np.ascontiguousarray(inputs[name])
        arrays[f"in_{name}_dram"] = a
        args.append(nc.dram_tensor(f"in_{name}_dram", a.shape, _mybir.dt.from_np(a.dtype), kind="ExternalInput").ap())
    for i, shape in enumerate(_OUTS):
        args.append(nc.dram_tensor(f"out_{i}_dram", shape, _mybir.dt.float32, kind="ExternalOutput").ap())
    build(nc, *args)
    r = _run(nc, [arrays], core_ids=[0])
    return tuple(r.results[0][f"out_{i}_dram"] for i in range(len(_OUTS)))
```
